# Optimizing a Trainium2 kernel written in Bass

```python
import jax, jax.numpy as jnp
from jax import lax
import numpy as np
import math

D_MODEL = 2048
BATCH = 1
SEQ = 256
DEPTH = 1

CHUNK = 64
PLE_DIM = 256
EPS = 1e-6

ATT_HEAD_DIM = 64
ATT_WIDTH = D_MODEL // 2
ATT_HEADS = ATT_WIDTH // ATT_HEAD_DIM
BAND_CHUNKS = 9
MAX_REL_DIST = 256

GLA_HEADS = 4
GLA_WIDTH = D_MODEL // 2
GLA_DV = GLA_WIDTH // GLA_HEADS
GLA_KEY_WIDTH = GLA_WIDTH // 2
GLA_DK = GLA_KEY_WIDTH // GLA_HEADS
GLA_GATE_RANK = 16
GLA_GATE_TAU = 16.0

MIX_WIDTH = ATT_WIDTH + GLA_WIDTH
IN_SPLITS = (ATT_WIDTH, ATT_WIDTH, ATT_WIDTH,
             GLA_KEY_WIDTH, GLA_KEY_WIDTH,
             GLA_WIDTH, GLA_WIDTH,
             GLA_GATE_RANK)
IN_PROJ_WIDTH = sum(IN_SPLITS)

D_FF = 5632
CONV_WIDTH = 3


def rms_norm(x, w):
    xf = x.astype(jnp.float32)
    y = xf * lax.rsqrt(jnp.mean(xf * xf, axis=-1, keepdims=True) + EPS)
    return (y * w.astype(jnp.float32)).astype(x.dtype)

def split_cols(t, sizes):
    idx = [int(v) for v in np.cumsum(sizes)[:-1]]
    return jnp.split(t, idx, axis=-1)

def rel_pos_bias(table):
    q_idx = jnp.arange(CHUNK) + (BAND_CHUNKS - 1) * CHUNK
    k_idx = jnp.arange(BAND_CHUNKS * CHUNK)
    dist = jnp.clip(q_idx[:, None] - k_idx[None, :], -MAX_REL_DIST, MAX_REL_DIST) + MAX_REL_DIST
    return table[:, dist]

def chunked_band_attention(q, k, v, bias_table):
    B, T, H, hd = q.shape
    nc = T // CHUNK
    pad = (BAND_CHUNKS - 1) * CHUNK
    band = BAND_CHUNKS * CHUNK
    k_pad = jnp.pad(k, ((0, 0), (pad, 0), (0, 0), (0, 0)))
    v_pad = jnp.pad(v, ((0, 0), (pad, 0), (0, 0), (0, 0)))
    bias = rel_pos_bias(bias_table).astype(jnp.float32)[None]
    key_off = jnp.arange(band) - pad
    q_chunks = q.reshape(B, nc, CHUNK, H, hd).transpose(1, 0, 2, 3, 4)
    scale = hd ** -0.5
    neg = jnp.finfo(jnp.float32).min

    def one_chunk(args):
        c, qc = args
        start = c * CHUNK
        kb = lax.dynamic_slice_in_dim(k_pad, start, band, axis=1)
        vb = lax.dynamic_slice_in_dim(v_pad, start, band, axis=1)
        s = jnp.einsum('bqhd,bkhd->bhqk', qc, kb).astype(jnp.float32) * scale + bias
        valid = (start + key_off) >= 0
        s = jnp.where(valid[None, None, None, :], s, neg)
        pr = jax.nn.softmax(s, axis=-1).astype(vb.dtype)
        return jnp.einsum('bhqk,bkhd->bqhd', pr, vb)

    out = lax.map(one_chunk, (jnp.arange(nc), q_chunks))
    return out.transpose(1, 0, 2, 3, 4).reshape(B, T, H * hd)

def gated_linear_attention(q, k, v, log_a):
    B, T, H, dk = q.shape
    dv = v.shape[-1]
    nc = T // CHUNK

    def to_chunks(t):
        return t.reshape(B, nc, CHUNK, H, t.shape[-1]).transpose(0, 1, 3, 2, 4).astype(jnp.float32)

    qc = to_chunks(q) * (dk ** -0.5)
    kc = to_chunks(k)
    vc = to_chunks(v)
    b = jnp.cumsum(to_chunks(log_a), axis=3)
    b_last = b[:, :, :, -1:, :]
    q_dec = qc * jnp.exp(b)
    k_inv = kc * jnp.exp(-b)
    k_to_end = kc * jnp.exp(b_last - b)
    causal = jnp.tril(jnp.ones((CHUNK, CHUNK), dtype=bool))
    attn = jnp.where(causal, jnp.einsum('bnhid,bnhjd->bnhij', q_dec, k_inv), 0.0)
    o_intra = jnp.einsum('bnhij,bnhjv->bnhiv', attn, vc)

    chunk_update = jnp.einsum('bnhjd,bnhjv->bnhdv', k_to_end, vc)
    chunk_decay = jnp.exp(b_last[:, :, :, 0, :])

    def step(S, xs):
        upd, dec = xs
        return dec[..., None] * S + upd, S

    S0 = jnp.zeros((B, H, dk, dv), jnp.float32)
    _, S_prev = lax.scan(step, S0, (chunk_update.transpose(1, 0, 2, 3, 4),
                                    chunk_decay.transpose(1, 0, 2, 3)))
    S_prev = S_prev.transpose(1, 0, 2, 3, 4)
    o_inter = jnp.einsum('bnhid,bnhdv->bnhiv', q_dec, S_prev)
    o = o_intra + o_inter
    return o.transpose(0, 1, 3, 2, 4).reshape(B, T, H, dv)

def causal_depthwise_conv(u, w, bias):
    T = u.shape[1]
    up = jnp.pad(u, ((0, 0), (CONV_WIDTH - 1, 0), (0, 0)))
    y = bias
    for tap in range(CONV_WIDTH):
        y = y + up[:, tap:tap + T] * w[tap]
    return y

def first_inputs(seed: int = 0) -> dict:
    key = jax.random.key(seed)
    ks = jax.random.split(key, 20)
    f32 = jnp.float32

    def nrm(k, shape, scale):
        return jax.random.normal(k, shape, f32) * scale

    def gain(k, shape):
        return 1.0 + 0.05 * jax.random.normal(k, shape, f32)

    return {
        "x": nrm(ks[0], (BATCH, SEQ, D_MODEL), 1.0),
        "p": nrm(ks[1], (DEPTH, BATCH, SEQ, PLE_DIM), 1.0),
        "norm_mix_w": gain(ks[2], (DEPTH, D_MODEL)),
        "w_in": nrm(ks[3], (DEPTH, D_MODEL, IN_PROJ_WIDTH), D_MODEL ** -0.5),
        "att_rel_bias": nrm(ks[4], (DEPTH, ATT_HEADS, 2 * MAX_REL_DIST + 1), 0.3),
        "w_gla_gate_up": nrm(ks[5], (DEPTH, GLA_GATE_RANK, GLA_KEY_WIDTH), GLA_GATE_RANK ** -0.5),
        "b_gla_gate": nrm(ks[6], (DEPTH, GLA_KEY_WIDTH), 0.5),
        "gla_norm_w": gain(ks[7], (DEPTH, GLA_DV)),
        "w_out": nrm(ks[8], (DEPTH, MIX_WIDTH, D_MODEL), MIX_WIDTH ** -0.5),
        "norm_ffn_w": gain(ks[9], (DEPTH, D_MODEL)),
        "w_ffn_up": nrm(ks[10], (DEPTH, D_MODEL, 2 * D_FF), D_MODEL ** -0.5),
        "w_ffn_conv": nrm(ks[11], (DEPTH, CONV_WIDTH, 2 * D_FF), CONV_WIDTH ** -0.5),
        "b_ffn_conv": nrm(ks[12], (DEPTH, 2 * D_FF), 0.02),
        "w_ffn_down": nrm(ks[13], (DEPTH, D_FF, D_MODEL), D_FF ** -0.5),
        "norm_ple_w": gain(ks[14], (DEPTH, D_MODEL)),
        "w_ple_gate": nrm(ks[15], (DEPTH, D_MODEL, D_MODEL), D_MODEL ** -0.5),
        "w_ple_proj": nrm(ks[16], (DEPTH, PLE_DIM, D_MODEL), PLE_DIM ** -0.5),
        "final_norm_w": gain(ks[17], (D_MODEL,)),
    }

def first_block(x, p, norm_mix_w, w_in, att_rel_bias, w_gla_gate_up, b_gla_gate, gla_norm_w,
              w_out, norm_ffn_w, w_ffn_up, w_ffn_conv, b_ffn_conv, w_ffn_down,
              norm_ple_w, w_ple_gate, w_ple_proj, final_norm_w):
    B, T, _ = x.shape
    for i in range(DEPTH):
        h = rms_norm(x, norm_mix_w[i])
        proj = h @ w_in[i]
        q_a, k_a, v_a, q_g, k_g, v_g, r_g, gate_lr = split_cols(proj, IN_SPLITS)

        hs_a = (B, T, ATT_HEADS, ATT_HEAD_DIM)
        y_a = chunked_band_attention(q_a.reshape(hs_a), k_a.reshape(hs_a), v_a.reshape(hs_a),
                                     att_rel_bias[i])

        gate_logit = (gate_lr @ w_gla_gate_up[i] + b_gla_gate[i]).astype(jnp.float32)
        log_a = (jax.nn.log_sigmoid(gate_logit) / GLA_GATE_TAU).reshape(B, T, GLA_HEADS, GLA_DK)
        o_g = gated_linear_attention(q_g.reshape(B, T, GLA_HEADS, GLA_DK),
                                     k_g.reshape(B, T, GLA_HEADS, GLA_DK),
                                     v_g.reshape(B, T, GLA_HEADS, GLA_DV), log_a)
        o_g = rms_norm(o_g.astype(x.dtype), gla_norm_w[i]).reshape(B, T, GLA_WIDTH)
        y_g = o_g * jax.nn.silu(r_g)

        x = x + jnp.concatenate([y_a, y_g], axis=-1) @ w_out[i]

        h = rms_norm(x, norm_ffn_w[i])
        u = causal_depthwise_conv(h @ w_ffn_up[i], w_ffn_conv[i], b_ffn_conv[i])
        u_gate, u_val = jnp.split(u, 2, axis=-1)
        x = x + (jax.nn.gelu(u_gate) * u_val) @ w_ffn_down[i]

        h = rms_norm(x, norm_ple_w[i])
        g = jax.nn.sigmoid(h @ w_ple_gate[i])
        x = x + g * (p[i] @ w_ple_proj[i])
    return rms_norm(x, final_norm_w)


HEAD_DIM = 64
A_Q_HEADS = 16
A_KV_HEADS = 4
A_GROUP = A_Q_HEADS // A_KV_HEADS
WINDOW = 128
B_HEADS = 16
BLOCK = 128
D_FF_2 = ((8 * D_MODEL // 3 + 255) // 256) * 256

A_Q_W = A_Q_HEADS * HEAD_DIM
A_KV_W = A_KV_HEADS * HEAD_DIM
B_W = B_HEADS * HEAD_DIM
IN_SPLITS_2 = (A_Q_W, A_KV_W, A_KV_W, B_W, B_W, B_W, D_MODEL, D_MODEL)
IN_WIDTH = sum(IN_SPLITS_2)
IN_OFFSETS = tuple(int(o) for o in np.cumsum(IN_SPLITS_2)[:-1])


def rmsnorm(x, g):
    xf = x.astype(jnp.float32)
    inv = lax.rsqrt(jnp.mean(xf * xf, axis=-1, keepdims=True) + EPS)
    return (xf * inv * g.astype(jnp.float32)).astype(x.dtype)

def alibi_slopes(n_heads):
    h = jnp.arange(1, n_heads + 1, dtype=jnp.float32)
    return jnp.exp2(-8.0 * h / n_heads)

def sliding_window_attention(q, k, v, sinks):
    B, S = q.shape[0], q.shape[1]
    nb = S // BLOCK
    qb = q.reshape(B, nb, BLOCK, A_KV_HEADS, A_GROUP, HEAD_DIM)
    kb = k.reshape(B, nb, BLOCK, A_KV_HEADS, HEAD_DIM)
    vb = v.reshape(B, nb, BLOCK, A_KV_HEADS, HEAD_DIM)
    pad_k = jnp.zeros_like(kb[:, :1])
    pad_v = jnp.zeros_like(vb[:, :1])
    kk = jnp.concatenate([jnp.concatenate([pad_k, kb[:, :-1]], axis=1), kb], axis=2)
    vv = jnp.concatenate([jnp.concatenate([pad_v, vb[:, :-1]], axis=1), vb], axis=2)

    scale = 1.0 / math.sqrt(HEAD_DIM)
    s = jnp.einsum('bnqhgd,bnkhd->bnhgqk', qb, kk).astype(jnp.float32) * scale

    qi = jnp.arange(BLOCK)[:, None]
    ki = jnp.arange(2 * BLOCK)[None, :]
    dist = (BLOCK + qi - ki)
    blk = jnp.arange(nb)[:, None, None]
    valid = (dist >= 0) & (dist < WINDOW)
    valid = valid[None] & ((blk > 0) | (ki[None] >= BLOCK))

    slopes = alibi_slopes(A_Q_HEADS).reshape(A_KV_HEADS, A_GROUP)
    s = s - slopes[:, :, None, None] * dist.astype(jnp.float32)[None, None]
    s = jnp.where(valid[None, :, None, None], s, -jnp.inf)

    sink = sinks.astype(jnp.float32).reshape(A_KV_HEADS, A_GROUP)[None, None, :, :, None, None]
    sink = jnp.broadcast_to(sink, s.shape[:-1] + (1,))
    p = jax.nn.softmax(jnp.concatenate([s, sink], axis=-1), axis=-1)[..., :-1]
    o = jnp.einsum('bnhgqk,bnkhd->bnqhgd', p.astype(v.dtype), vv)
    return o.reshape(B, S, A_Q_W)

def stick_breaking_attention(q, k, v):
    B, S = q.shape[0], q.shape[1]
    nb = S // BLOCK
    scale = 1.0 / math.sqrt(HEAD_DIM)
    qb = q.reshape(B, nb, BLOCK, B_HEADS, HEAD_DIM).transpose(1, 0, 2, 3, 4)
    kpos = jnp.arange(S)

    def one_block(args):
        qblk, i = args
        z = jnp.einsum('bqhd,bkhd->bhqk', qblk, k).astype(jnp.float32) * scale
        tpos = i * BLOCK + jnp.arange(BLOCK)
        causal = kpos[None, :] < tpos[:, None]
        log_beta = jax.nn.log_sigmoid(z)
        log_fail = jnp.where(causal, jax.nn.log_sigmoid(-z), 0.0)
        suffix = lax.cumsum(log_fail, axis=3, reverse=True) - log_fail
        a = jnp.where(causal, jnp.exp(log_beta + suffix), 0.0)
        return jnp.einsum('bhqk,bkhd->bqhd', a.astype(v.dtype), v)

    o = lax.map(one_block, (qb, jnp.arange(nb)))
    return o.transpose(1, 0, 2, 3, 4).reshape(B, S, B_W)

def swiglu(h, w_in, w_down):
    gu = h @ w_in
    gate, up = jnp.split(gu, 2, axis=-1)
    return (jax.nn.silu(gate) * up) @ w_down

def second_inputs(seed: int = 0) -> dict:
    key = jax.random.key(seed)
    ks = jax.random.split(key, 12)
    f32 = jnp.float32

    def w(k, shape, fan_in):
        return jax.random.normal(k, shape, f32) * (fan_in ** -0.5)

    def gain(k, shape):
        return 1.0 + 0.02 * jax.random.normal(k, shape, f32)

    return {
        "x": jax.random.normal(ks[0], (BATCH, SEQ, D_MODEL), f32),
        "norm_mix_g": gain(ks[1], (DEPTH, D_MODEL)),
        "w_in": w(ks[2], (DEPTH, D_MODEL, IN_WIDTH), D_MODEL),
        "sink_logits": 0.5 * jax.random.normal(ks[3], (DEPTH, A_Q_HEADS), f32),
        "w_branch_a": w(ks[4], (DEPTH, A_Q_W, D_MODEL), A_Q_W),
        "w_branch_b": w(ks[5], (DEPTH, B_W, D_MODEL), B_W),
        "w_out": w(ks[6], (DEPTH, D_MODEL, D_MODEL), D_MODEL),
        "norm_ffn_g": gain(ks[7], (DEPTH, D_MODEL)),
        "w_ffn_in": w(ks[8], (DEPTH, D_MODEL, 2 * D_FF_2), D_MODEL),
        "w_ffn_down": w(ks[9], (DEPTH, D_FF_2, D_MODEL), D_FF_2),
        "norm_final_g": gain(ks[10], (D_MODEL,)),
    }

def second_block(x, norm_mix_g, w_in, sink_logits, w_branch_a, w_branch_b, w_out,
              norm_ffn_g, w_ffn_in, w_ffn_down, norm_final_g):
    B, S, _ = x.shape
    for layer in range(DEPTH):
        h = rmsnorm(x, norm_mix_g[layer])
        proj = h @ w_in[layer]
        qa, ka, va, qb, kb, vb, ga, gb = jnp.split(proj, IN_OFFSETS, axis=-1)

        ya = sliding_window_attention(
            qa.reshape(B, S, A_Q_HEADS, HEAD_DIM),
            ka.reshape(B, S, A_KV_HEADS, HEAD_DIM),
            va.reshape(B, S, A_KV_HEADS, HEAD_DIM),
            sink_logits[layer]) @ w_branch_a[layer]
        yb = stick_breaking_attention(
            qb.reshape(B, S, B_HEADS, HEAD_DIM),
            kb.reshape(B, S, B_HEADS, HEAD_DIM),
            vb.reshape(B, S, B_HEADS, HEAD_DIM)) @ w_branch_b[layer]

        merged = jax.nn.sigmoid(ga) * ya + jax.nn.sigmoid(gb) * yb
        x = x + merged @ w_out[layer]
        x = x + swiglu(rmsnorm(x, norm_ffn_g[layer]), w_ffn_in[layer], w_ffn_down[layer])
    return rmsnorm(x, norm_final_g)


def setup_inputs(seed=0):
    out = dict(first_inputs(seed))
    for name, value in second_inputs(seed + 1).items():
        if name != "x":
            out[name + "_2"] = value
    return out


def reference(
    x, p, norm_mix_w, w_in, att_rel_bias, w_gla_gate_up, b_gla_gate, gla_norm_w, w_out,
    norm_ffn_w, w_ffn_up, w_ffn_conv, b_ffn_conv, w_ffn_down, norm_ple_w, w_ple_gate,
    w_ple_proj, final_norm_w, norm_mix_g_2, w_in_2, sink_logits_2, w_branch_a_2, w_branch_b_2,
    w_out_2, norm_ffn_g_2, w_ffn_in_2, w_ffn_down_2, norm_final_g_2,
):
    x = first_block(
        x, p, norm_mix_w, w_in, att_rel_bias, w_gla_gate_up, b_gla_gate, gla_norm_w, w_out,
        norm_ffn_w, w_ffn_up, w_ffn_conv, b_ffn_conv, w_ffn_down, norm_ple_w, w_ple_gate,
        w_ple_proj, final_norm_w,
    )
    return second_block(
        x, norm_mix_g_2, w_in_2, sink_logits_2, w_branch_a_2, w_branch_b_2, w_out_2,
        norm_ffn_g_2, w_ffn_in_2, w_ffn_down_2, norm_final_g_2,
    )


_drawn_inputs = setup_inputs


def setup_inputs(seed=0):
    import zlib

    import numpy as np

    out = dict(_drawn_inputs(seed))
    spreads = {}
    factors = {'b_ffn_conv': 3.537,
     'norm_ple_w': 6.219,
     'norm_mix_g_2': 5.25,
     'sink_logits_2': 34.841,
     'norm_ffn_g_2': 4.071,
     'norm_final_g_2': 7.633}
    for name, (base, spread) in spreads.items():
        noise = np.random.default_rng([zlib.crc32(name.encode()), seed]).standard_normal(out[name].shape)
        drawn = base * np.exp(spread * noise) if base else spread * noise
        out[name] = __import__('jax').numpy.asarray(drawn.astype(out[name].dtype))
    for name, factor in factors.items():
        out[name] = (out[name] * factor).astype(out[name].dtype)
    return out
```

```python
from contextlib import ExitStack

import concourse.bass as bass
from concourse import mybir


F32 = mybir.dt.float32
F32R = mybir.dt.float32r
ACT = mybir.ActivationFunctionType
ALU = mybir.AluOpType
AXX = mybir.AxisListType.X

P = 128
T = 256
TB = T // P
D = 2048
KT = D // P
NT = 512
EPS = 1e-6
RING = 4
CHUNK_KT = 2

HD = 64
HEADS = 16
PAIRS = HEADS // 2
MAX_REL = 256
ATT_W = HEADS * HD
GLA_HEADS = 4
GLA_DK = 128
GLA_DV = 256
GLA_KW = GLA_HEADS * GLA_DK
GLA_W = GLA_HEADS * GLA_DV
RANK = 16
TAU = 16.0
LOOK = 64
QA1, KA1, VA1 = 0, ATT_W, 2 * ATT_W
QG1 = 3 * ATT_W
KG1 = QG1 + GLA_KW
VG1 = KG1 + GLA_KW
RG1 = VG1 + GLA_W
GATE1 = RG1 + GLA_W
FF = 5632
FKT = FF // P

KV_HEADS = 4
GROUP = HEADS // KV_HEADS
WINDOW = 128
QA2, KA2, VA2 = 0, 1024, 1280
QB2, KB2, VB2 = 1536, 2560, 3584
GATES2 = 4608

C_IN1 = 0
C_OUT1 = C_IN1 + GATE1 // NT * 8
C_UP1 = C_OUT1 + D // NT * 8
C_DOWN1 = C_UP1 + 2 * FF // NT * 8
C_PROJ = C_DOWN1 + D // NT * FKT // 2
C_PLE = C_PROJ + D // NT
C_IN2 = C_PLE + D // NT * 8
C_BR = C_IN2 + 8704 // NT * 8
C_OUT2 = C_BR + D // NT * 8
C_UP2 = C_OUT2 + D // NT * 8
C_DOWN2 = C_UP2 + 2 * FF // NT * 8
C_END = C_DOWN2 + D // NT * FKT // 2

A_IN1 = 1
A_OUT1 = A_IN1 + 6
A_UP1 = A_OUT1 + 2
A_DOWN1 = A_UP1 + 11
A_PROJ = A_DOWN1 + 2
A_PLE = A_PROJ + 2
A_IN2 = A_PLE + 2
A_BR = (A_IN2 + 9, A_IN2 + 8)
A_OUT2 = (A_BR[0] + 4, A_BR[1] + 4)
A_UP2 = (A_OUT2[0] + 2, A_OUT2[1] + 2)
A_DOWN2 = (A_UP2[0] + 11, A_UP2[1] + 11)

G_X1 = 0
G_Y1 = G_X1 + 8
G_F1 = G_Y1 + 8
G_P = G_F1 + 8
G_PLE = G_P + 1
G_X2 = G_PLE + 8
G_Y2 = G_X2 + 8
G_M2 = G_Y2 + 8
G_F2 = G_M2 + 8

X_PLE, X_NORM, X_FINAL = 0, 4, 8

N_IN1, N_F1, N_PLE, N_END1, N_IN2, N_F2, N_END2 = range(7)

GV_NEG = 4
GV_LA = GV_NEG + 2
GV_KE = GV_LA + 9
GV_ST1 = GV_KE + 4
GV_ST2 = GV_ST1 + 8
GV_OSM = GV_ST2 + 1
GV_END = GV_OSM + 11
GA_ATTN = 5

SCORES_FREE = 3 * P
NEG = -1e30
MASKED = -3e38


def pair(v, p):
    return v[p] if isinstance(v, tuple) else v


def two_blocks_kernel(nc, x, p, norm_mix_w, w_in, rel_bias, w_gate_up, b_gate, gla_norm_w, w_out, norm_ffn_w,
                      w_up, w_conv, b_conv, w_down, norm_ple_w, w_ple_gate, w_ple_proj, final_w,
                      norm_mix_g2, w_in2, sinks, w_bra, w_brb, w_out2, norm_ffn_g2, w_up2, w_down2, final_g2, out):
    ctx = ExitStack()
    with ctx:
        def sem(name):
            return ctx.enter_context(nc.semaphore(name))

        place = [nc.sbuf_base + (-nc.sbuf_base) % 64]

        def sb(name, shape, dt=F32, at=None):
            size = 4
            for n in shape[1:]:
                size *= n
            size += -size % 64
            if at is None:
                at = place[0]
                place[0] += size
            else:
                ends.append(at + size)
            return nc.alloc_sbuf_tensor_at(name, shape, dt, offset=at)

        ends = []
        X = sb("X", [P, TB, D])
        AH = sb("AH", [P, KT, T], F32R)
        AL = sb("AL", [P, KT, T], F32R)
        WR = sb("WR", [P, RING, CHUNK_KT, NT])
        WH = sb("WH", [P, RING, CHUNK_KT, NT], F32R)
        WL = sb("WL", [P, RING, CHUNK_KT, NT], F32R)
        ident = sb("ident", [P, P])
        tri_le = sb("tri_le", [P, P])
        tri_gt = sb("tri_gt", [P, P])
        neg_tri = sb("neg_tri", [P, P])
        neg_ones = sb("neg_ones", [P, P])
        neg_mask = sb("neg_mask", [P, P])
        vec = sb("vec", [P, 5 * KT + 4 * 2 * FKT])
        nw = vec[:, 0:5 * KT].rearrange("p (n k) -> p n k", k=KT)
        cw = vec[:, 5 * KT:].rearrange("p (n k) -> p n k", k=2 * FKT)
        junk = sb("junk", [P, NT])
        ss = sb("ss", [P, TB, 4])
        ssum = sb("ssum", [P, TB])
        smean = sb("smean", [P, TB])
        sroot = sb("sroot", [P, TB])
        inv = sb("inv", [P, 7, TB])
        base = place[0]
        P1 = sb("P1", [P, TB, GATE1], at=base)
        o1 = base + TB * GATE1 * 4
        BIAS = sb("BIAS", [P, HEADS, 3 * P], at=o1)
        QK = sb("QK", [P, PAIRS, 2, T], at=o1 + 24576)
        o2 = o1 + 24576 + 16384
        SB = sb("SB", [P, 2, SCORES_FREE], at=o2)
        PB = sb("PB", [P, 2, SCORES_FREE], at=o2 + 3072)
        PT = sb("PT", [P, 2, SCORES_FREE], at=o2 + 6144)
        nmax = sb("nmax", [P, HEADS, 2], at=o2 + 9216)
        rsum = sb("rsum", [P, HEADS, 2], at=o2 + 9344)
        rrec = sb("rrec", [P, HEADS, 2], at=o2 + 9472)
        rmax = sb("rmax", [P, HEADS, 2], at=o2 + 9600)
        glT = sb("glT", [RANK, T], at=o1 + 51200)
        wgu = sb("wgu", [RANK, GLA_KW], at=o1 + 1024)
        bgb = sb("bgb", [P, GLA_KW], at=o1 + 3072)
        LG = sb("LG", [P, TB, GLA_KW], at=o1 + 5120)
        LE = sb("LE", [P, TB, GLA_KW], at=o1 + 9216)
        LA = sb("LA", [P, TB, GLA_KW], at=o1 + 13312)
        EB = sb("EB", [P, GLA_HEADS, T], at=o1 + 17408)
        EN = sb("EN", [P, GLA_HEADS, T], at=o1 + 21504)
        QD = sb("QD", [P, GLA_HEADS, T], at=o1 + 25600)
        KI = sb("KI", [P, GLA_HEADS, T], at=o1 + 29696)
        KE = sb("KE", [P, TB, GLA_KW], at=o1 + 33792)
        AT = sb("AT", [P, TB * GLA_HEADS, P], at=o1 + 37888)
        ST = sb("ST", [P, 3, GLA_HEADS, GLA_DV], at=o1 + 41984)
        gnw = sb("gnw", [P, GLA_DV], at=o1 + 5120)
        osq = sb("osq", [P, TB, GLA_HEADS], at=o1 + 6144)
        osm = sb("osm", [P, TB, GLA_HEADS], at=o1 + 6208)
        osr = sb("osr", [P, TB, GLA_HEADS], at=o1 + 6272)
        oiv = sb("oiv", [P, TB, GLA_HEADS], at=o1 + 6336)
        SR = sb("SR", [P, TB, GLA_W], at=o1 + 9216)
        WG = sb("WG", [P, KT, RANK], at=o1 + 54400)
        WGH = sb("WGH", [P, KT * RANK + P - RANK], F32R, at=o1 + 41984)
        WGL = sb("WGL", [P, KT * RANK + P - RANK], F32R, at=o1 + 43520)
        ZH = sb("ZH", [P, KT, T], F32R, at=o1)
        ZL = sb("ZL", [P, KT, T], F32R, at=o1 + 16384)
        BH = sb("BH", [P, FKT, T], F32R, at=base)
        BL = sb("BL", [P, FKT, T], F32R, at=base + FKT * T * 4)
        o3 = base + 2 * FKT * T * 4
        U = sb("U", [P, 2, TB, NT], at=o3)
        CV = sb("CV", [P, 2, 4, T], at=o3 + 8192)
        SG = sb("SG", [P, TB, NT], at=o3)
        HB = sb("HB", [P, TB, NT], at=o3 + 4096)
        pin = sb("pin", [P, TB, T], at=o3)
        PTH = sb("PTH", [P, CHUNK_KT, T], F32R, at=o3 + 2048)
        PTL = sb("PTL", [P, CHUNK_KT, T], F32R, at=o3 + 4096)
        fw2 = sb("fw2", [P, D], at=o3)
        norm_rows = sb("norm_rows", [5 * KT, P], at=base)
        conv_rows = sb("conv_rows", [2 * FKT, 4, P], at=base + 512)
        PP = sb("PP", [P, TB, D], at=base)
        GT = sb("GT", [P, TB, NT], at=base + 16384)
        fw = sb("fw", [P, D], at=base + 20480)
        PQ = sb("PQ", [P, TB, GATES2], at=base)
        PG = sb("PG", [P, TB, 2 * D], at=base + TB * GATES2 * 4)
        o4 = base + TB * GATES2 * 4 + TB * 2 * D * 4
        QT2 = sb("QT2", [P, PAIRS, T], at=o4)
        KD = sb("KD", [P, TB, KV_HEADS, 2, HD], at=o4 + 8192)
        KT2 = sb("KT2", [P, KV_HEADS, T], at=o4 + 12288)
        SB2 = sb("SB2", [P, 2, SCORES_FREE], at=o4 + 16384)
        PB2 = sb("PB2", [P, 2, SCORES_FREE], at=o4 + 19456)
        PT2 = sb("PT2", [P, 2, SCORES_FREE], at=o4 + 22528)
        nmax2 = sb("nmax2", [P, HEADS, 2], at=o4 + 25600)
        rsum2 = sb("rsum2", [P, HEADS, 2], at=o4 + 25728)
        rrec2 = sb("rrec2", [P, HEADS, 2], at=o4 + 25856)
        rmax2 = sb("rmax2", [P, HEADS, 2], at=o4 + 25984)
        sk = sb("sk", [P, HEADS], at=o4 + 26112)
        sk2 = sb("sk2", [P, HEADS, 2], at=o4 + 26176)
        dist = sb("dist", [P, 2 * P], at=o4 + 26304)
        QKB = sb("QKB", [P, PAIRS, 2, T], at=o4)
        SM = sb("SM", [P, 4, SCORES_FREE], at=o4 + 16384)
        SE = sb("SE", [P, 4, SCORES_FREE], at=o4 + 22528)
        SA = sb("SA", [P, 2, SCORES_FREE], at=o4 + 28672)
        MH = sb("MH", [P, KT, T], F32R, at=base)
        ML = sb("ML", [P, KT, T], F32R, at=base + 16384)
        assert max(ends) <= nc.sbuf_usable_end, (max(ends), nc.sbuf_usable_end)

        acc = ctx.enter_context(nc.psum_tensor("acc", [P, 2, TB, NT], F32))
        tp = ctx.enter_context(nc.psum_tensor("tp", [P, 4, NT], F32))

        def acc_bank(n):
            return acc[:, n // 2, n % 2, :]

        w_loaded = [sem(f"w_loaded{s}") for s in range(RING)]
        hi_done, lo_done, chunk_used = sem("hi_done"), sem("lo_done"), sem("chunk_used")
        acc_free = [sem("acc_free0"), sem("acc_free1")]
        turned, turned_hi, turned_lo = sem("turned"), sem("turned_hi"), sem("turned_lo")
        x_in, x_scaled, squared, sums, mean, root, inv_ready = (
            sem("x_in"), sem("x_scaled"), sem("squared"), sem("sums"), sem("mean"), sem("root"), sem("inv_ready"))
        consts_in, masks, mask_step = sem("consts_in"), sem("masks"), sem("mask_step")
        bias_in, bias_masked = sem("bias_in"), sem("bias_masked")
        qk_turned, qk_copied, qk_copied_v = sem("qk_turned"), sem("qk_copied"), sem("qk_copied_v")
        s_full, s_read, s_max, s_neg, e_done, pt_full, pt_copied, pv_done = (
            sem("s_full"), sem("s_read"), sem("s_max"), sem("s_neg"), sem("e_done"), sem("pt_full"),
            sem("pt_copied"), sem("pv_done"))
        rec_done, y_ready = sem("rec_done"), sem("y_ready")
        gate_in, gate_pad, gate_hi, gate_lo, gate_pe, gate_v, gate_a = (
            sem("gate_in"), sem("gate_pad"), sem("gate_hi"), sem("gate_lo"), sem("gate_pe"), sem("gate_v"),
            sem("gate_a"))
        gla_pe, gla_v, gla_a, gla_p, gla_in = sem("gla_pe"), sem("gla_v"), sem("gla_a"), sem("gla_p"), sem("gla_in")
        p_in, vec_turned, vec_ready = sem("p_in"), sem("vec_turned"), sem("vec_ready")
        u_turned, c_init, tap1, conv_done, gelu_done, h_ready, h_hi, h_lo = (
            sem("u_turned"), sem("c_init"), sem("tap1"), sem("conv_done"), sem("gelu_done"),
            sem("h_ready"), sem("h_hi"), sem("h_lo"))
        hb_turned, hb_hi, hb_lo, g_mul = sem("hb_turned"), sem("hb_hi"), sem("hb_lo"), sem("g_mul")
        fw_in, sk_in, kd_done, sink_v, sink_a = sem("fw_in"), sem("sk_in"), sem("kd_done"), sem("sink_v"), sem("sink_a")
        z_full, m_done, z_read, ez_done, ln_done, sp_done, arg_full, a_done, stick_pv = (
            sem("z_full"), sem("m_done"), sem("z_read"), sem("ez_done"), sem("ln_done"), sem("sp_done"),
            sem("arg_full"), sem("a_done"), sem("stick_pv"))

        def slices_of(count):
            return lambda n: (acc_free[n % 2], pair(count, n % 2) + n // 2 + 1)

        def slices_scaled(first):
            return lambda n: (x_scaled, first + n + 1)

        sg_done, m_ready = sem("sg_done"), sem("m_ready")
        fg_in, out_done = sem("fg_in"), sem("out_done")

        block = ctx.enter_context(nc.Block())

        def wide(v, shape):
            return v.to_broadcast(shape)

        def rows(w, kt, cols):
            return w[kt * P:(kt + CHUNK_KT) * P, cols].rearrange("(a p) n -> p a n", p=P)

        def by_row(v):
            return v.rearrange("(k p) -> k p", p=P)

        @block.sync
        def _(sp):
            def load(w, kt, cols, base, j, it=None, per=0):
                n = base + j
                first = it is None and n < RING
                at = n if it is None else n + per * it
                if not first:
                    sp.wait_ge(hi_done, at - RING + 1)
                    sp.wait_ge(lo_done, at - RING + 1)
                sp.dma_start(WR[:, n % RING], rows(w, kt, cols)).then_inc(w_loaded[n % RING], 16)

            def tile(w, col, nk, base, j0, it=None, per=0, kt0=0):
                for q in range(nk // CHUNK_KT):
                    load(w, kt0 + CHUNK_KT * q, bass.ds(col, NT), base, j0 + q, it, per)

            def plain(w, base, n0, n1):
                with sp.Fori(n0, n1) as n:
                    tile(w, n * NT, KT, base, 0, n, 8)

            for tb in range(TB):
                sp.dma_start(X[:, tb], x[tb * P:(tb + 1) * P, :]).then_inc(x_in, 16)
            tile(w_in, 0, KT, C_IN1, 0)
            plain(w_in, C_IN1, 1, GATE1 // NT)
            plain(w_out, C_OUT1, 0, D // NT)
            with sp.Fori(0, FF // NT) as n:
                tile(w_up, n * NT, KT, C_UP1, 0, n, 16)
                tile(w_up, n * NT + FF, KT, C_UP1, 8, n, 16)
            with sp.Fori(0, D // NT // 2) as n:
                for half in range(2):
                    tile(w_down, n * (2 * NT) + half * NT, FKT, C_DOWN1, half * FKT // 2, n, FKT)
            for n in range(D // NT):
                load(w_ple_proj, 0, bass.ds(n * NT, NT), C_PROJ, n)
            plain(w_ple_gate, C_PLE, 0, D // NT)
            plain(w_in2, C_IN2, 0, 8704 // NT)
            with sp.Fori(0, D // NT) as n:
                tile(w_bra, n * NT, KT // 2, C_BR, 0, n, 8)
                tile(w_brb, n * NT, KT // 2, C_BR, 4, n, 8)
            plain(w_out2, C_OUT2, 0, D // NT)
            with sp.Fori(0, FF // NT) as n:
                tile(w_up2, n * NT, KT, C_UP2, 0, n, 16)
                tile(w_up2, n * NT + FF, KT, C_UP2, 8, n, 16)
            with sp.Fori(0, D // NT // 2) as n:
                for half in range(2):
                    tile(w_down2, n * (2 * NT) + half * NT, FKT, C_DOWN2, half * FKT // 2, n, FKT)
            for n in range(D // NT):
                sp.wait_ge(x_scaled, X_FINAL + n + 1)
                sp.dma_start(out[:, n * NT:(n + 1) * NT].rearrange("(a p) n -> p a n", p=P),
                             X[:, :, n * NT:(n + 1) * NT]).then_inc(out_done, 16)
            sp.wait_ge(out_done, 16 * (D // NT))

        @block.gpsimd
        def _(pool):
            for n, w in enumerate((norm_mix_w, norm_ffn_w, norm_ple_w, norm_mix_g2, norm_ffn_g2)):
                pool.dma_start(norm_rows[n * KT:(n + 1) * KT, :], by_row(w)).then_inc(consts_in, 16)
            for tap in range(3):
                pool.dma_start(conv_rows[:, tap], by_row(w_conv[tap])).then_inc(consts_in, 16)
            pool.dma_start(conv_rows[:, 3], by_row(b_conv)).then_inc(consts_in, 16)
            pool.dma_start(BIAS[:], bass.AP(tensor=rel_bias.tensor, offset=1,
                                            ap=[[1, P], [2 * MAX_REL + 1, HEADS], [1, 3 * P]])).then_inc(bias_in, 16)
            pool.dma_start(WG[:], w_in[:, GATE1:GATE1 + RANK].rearrange("(k p) n -> p k n", p=P)).then_inc(gate_in, 16)
            pool.memset(ident[:], 0.0).then_inc(mask_step, 1)
            pool.memset(tri_le[:], 1.0).then_inc(mask_step, 1)
            pool.memset(tri_gt[:], 1.0).then_inc(mask_step, 1)
            pool.memset(neg_tri[:], -1.0).then_inc(mask_step, 1)
            pool.memset(neg_mask[:], 0.0).then_inc(mask_step, 1)
            pool.memset(neg_ones[:], -1.0).then_inc(masks, 1)
            pool.wait_ge(mask_step, 5)
            pool.affine_select(out=ident[:], in_=ident[:], compare_op=ALU.not_equal, fill=1.0, base=0,
                               pattern=[[-1, P]], channel_multiplier=1).then_inc(masks, 1)
            pool.affine_select(out=neg_tri[:], in_=neg_tri[:], compare_op=ALU.is_ge, fill=0.0, base=0,
                               pattern=[[-1, P]], channel_multiplier=1).then_inc(masks, 1)
            pool.affine_select(out=neg_mask[:], in_=neg_mask[:], compare_op=ALU.is_ge, fill=NEG, base=-1,
                               pattern=[[1, P]], channel_multiplier=-1).then_inc(masks, 1)
            pool.affine_select(out=tri_le[:], in_=tri_le[:], compare_op=ALU.is_ge, fill=0.0, base=0,
                               pattern=[[1, P]], channel_multiplier=-1).then_inc(mask_step, 1)
            pool.affine_select(out=tri_gt[:], in_=tri_gt[:], compare_op=ALU.is_ge, fill=0.0, base=-1,
                               pattern=[[-1, P]], channel_multiplier=1).then_inc(mask_step, 1)
            pool.wait_ge(mask_step, 7)
            pool.memset(tri_le[0:LOOK, LOOK:P], 0.0).then_inc(masks, 1)
            pool.memset(tri_gt[LOOK:P, 0:LOOK], 0.0).then_inc(masks, 1)
            pool.wait_ge(bias_in, 16)
            pool.memset(BIAS[0:LOOK, :, P:P + LOOK], MASKED).then_inc(bias_masked, 1)
            pool.wait_ge(y_ready, 4)
            pool.dma_start(wgu[:], w_gate_up).then_inc(gla_in, 16)
            pool.dma_start(bgb[:], b_gate.partition_broadcast(P)).then_inc(gla_in, 16)
            pool.memset(AT[:], 0.0).then_inc(gla_p, 1)
            pool.wait_ge(gla_a, GA_ATTN)
            pool.affine_select(out=AT[:], in_=AT[:], compare_op=ALU.is_ge, fill=0.0, base=0,
                               pattern=[[0, TB * GLA_HEADS], [1, P]], channel_multiplier=-1).then_inc(gla_p, 1)
            pool.dma_start(gnw[:], gla_norm_w.partition_broadcast(P)).then_inc(gla_in, 16)
            pool.wait_ge(h_lo, FF // NT)
            pool.dma_start(pin[:], p.rearrange("(a p) n -> p a n", p=P)).then_inc(p_in, 16)
            pool.wait_ge(chunk_used, C_PROJ)
            pool.dma_start(fw[:], final_w.partition_broadcast(P)).then_inc(fw_in, 16)
            pool.wait_ge(acc_free[0], A_BR[0])
            pool.wait_ge(acc_free[1], A_BR[1])
            pool.dma_start(sk[:], sinks.partition_broadcast(P)).then_inc(sk_in, 16)
            pool.iota(dist[:], pattern=[[-1, 2 * P]], base=P, channel_multiplier=1,
                      allow_small_or_imprecise_dtypes=True).then_inc(kd_done, 1)
            pool.wait_ge(kd_done, 1)
            pool.affine_select(out=dist[:], in_=dist[:], compare_op=ALU.is_ge, fill=-NEG, base=P,
                               pattern=[[-1, 2 * P]], channel_multiplier=1).then_inc(kd_done, 1)
            pool.wait_ge(kd_done, 2)
            pool.affine_select(out=dist[:], in_=dist[:], compare_op=ALU.is_ge, fill=-NEG, base=-1,
                               pattern=[[1, 2 * P]], channel_multiplier=-1).then_inc(kd_done, 1)
            for tb in range(TB):
                for twin in range(2):
                    pool.tensor_copy(KD[:, tb, :, twin, :], PQ[:, tb, KA2:KA2 + KV_HEADS * HD]
                                     .rearrange("p (g d) -> p g d", d=HD)).then_inc(kd_done, 1)

            pool.wait_ge(hb_lo, 2 * (FF // NT))
            pool.dma_start(fw2[:], final_g2.partition_broadcast(P)).then_inc(fg_in, 16)

        @block.tensor
        def _(pe):
            def chunk(H, L, kt, base, j, a, first, last, it=None, per=0):
                n = base + j
                pe.wait_ge(lo_done, (n if it is None else n + per * it) + 1)
                for k in range(CHUNK_KT):
                    for tb in range(TB):
                        cols = slice(tb * P, (tb + 1) * P)
                        o, s = acc[:, a, tb, :], n % RING
                        begin, end = first and k == 0, last and k == CHUNK_KT - 1
                        pe.matmul(o, H[:, kt + k, cols], WH[:, s, k], start=begin, stop=False)
                        pe.matmul(o, H[:, kt + k, cols], WL[:, s, k], start=False, stop=False)
                        mm = pe.matmul(o, L[:, kt + k, cols], WH[:, s, k], start=False, stop=end)
                mm.then_inc(chunk_used, 1)

            def tile(H, L, nk, base, j0, a, count, it=None, per=0, each=1, kt0=0, between=None, groups=None):
                pe.wait_ge(acc_free[a], count if it is None else count + each * it)
                for q in range(nk // CHUNK_KT):
                    if groups is not None:
                        pe.wait_ge(turned_lo, groups + kt0 // 2 + q + 1)
                    chunk(H, L, kt0 + CHUNK_KT * q, base, j0 + q, a, q == 0, q == nk // CHUNK_KT - 1, it, per)
                    if between is not None and q == 1:
                        between()

            def turn(src, nkt, group):
                for g in range(nkt // 2):
                    n = group + g
                    if n >= 4:
                        pe.wait_ge(turned_lo, n - 3)
                    for k in range(2):
                        for tb in range(TB):
                            mm = pe.transpose(tp[:, n % 4, k * T + tb * P:k * T + (tb + 1) * P],
                                              src(2 * g + k, tb), ident[:])
                    mm.then_inc(turned, 1)

            def x_cols(kt, tb):
                return X[:, tb, kt * P:(kt + 1) * P]

            def turn_x(ready, group):
                for g in range(KT // 2):
                    n = group + g
                    if g % 2 == 0:
                        pe.wait_ge(*ready(g // 2))
                    if n >= 4:
                        pe.wait_ge(turned_lo, n - 3)
                    for k in range(2):
                        for tb in range(TB):
                            mm = pe.transpose(tp[:, n % 4, k * T + tb * P:k * T + (tb + 1) * P],
                                              x_cols(2 * g + k, tb), ident[:])
                    mm.then_inc(turned, 1)

            def two_tiles(H, L, base, count, n_it, nk, groups=None):
                per = nk
                with pe.Fori(0, n_it) as i:
                    tile(H, L, nk, base, 0, 0, pair(count, 0), i, per, groups=groups)
                    tile(H, L, nk, base, nk // 2, 1, pair(count, 1), i, per, groups=groups)

            def scores(h, n, q_of, k_of):
                if n >= 2:
                    pe.wait_ge(s_read, n - 1)
                o = tp[:, n % 2, :]
                pe.matmul(o[:, 0:P], q_of(h, 0, P), k_of(h, 0, P), start=True, stop=True)
                pe.matmul(o[:, P:3 * P], q_of(h, P, T), k_of(h, 0, T), start=True, stop=True).then_inc(s_full, 1)

            def turn_weights(n, B):
                pe.wait_ge(e_done, n + 1)
                if n >= 2:
                    pe.wait_ge(pt_copied, n - 1)
                for b in range(3):
                    mm = pe.transpose(tp[:, 2 + n % 2, b * P:(b + 1) * P], B[:, n % 2, b * P:(b + 1) * P], ident[:])
                mm.then_inc(pt_full, 1)

            def weigh(h, n, B, v_of):
                pe.wait_ge(pt_copied, n + 1)
                for qb in range(TB):
                    o = acc_bank(2 * qb + h // 8)[:, (h % 8) * HD:(h % 8 + 1) * HD]
                    for kb in range(qb + 1):
                        blk = qb + kb
                        mm = pe.matmul(o, B[:, n % 2, blk * P:(blk + 1) * P], v_of(h, kb),
                                       start=(kb == 0), stop=(kb == qb))
                mm.then_inc(pv_done, 1)

            def softmax_attention(n0, q_of, k_of, v_of, EXP, TURNED):
                scores(0, n0, q_of, k_of)
                scores(1, n0 + 1, q_of, k_of)
                for h in range(HEADS):
                    turn_weights(n0 + h, EXP)
                    if h + 2 < HEADS:
                        scores(h + 2, n0 + h + 2, q_of, k_of)
                    weigh(h, n0 + h, TURNED, v_of)

            pe.wait_ge(masks, 6)
            pe.wait_ge(consts_in, 16 * 9)
            pe.transpose(acc_bank(3)[:, 0:5 * KT], norm_rows[:], ident[0:5 * KT, 0:5 * KT])
            for n in range(4):
                mm = pe.transpose(acc_bank(3)[:, 5 * KT + n * 2 * FKT:5 * KT + (n + 1) * 2 * FKT], conv_rows[:, n, :],
                                  ident[0:2 * FKT, 0:2 * FKT])
            mm.then_inc(vec_turned, 1)
            pe.wait_ge(x_in, 16 * TB)
            turn(x_cols, KT, G_X1)
            tile(AH, AL, KT, C_IN1, 0, 0, A_IN1, groups=G_X1)
            tile(AH, AL, KT, C_IN1, 8, 1, A_IN1)
            with pe.Fori(1, GATE1 // NT // 2) as i:
                tile(AH, AL, KT, C_IN1, 0, 0, A_IN1, i, 16)
                tile(AH, AL, KT, C_IN1, 8, 1, A_IN1, i, 16)
            pe.wait_ge(gate_lo, 1)
            for k in range(KT):
                cols = slice(k * RANK, k * RANK + P)
                pe.matmul(tp[:, 0, 0:T], WGH[:, cols], AH[:, k], start=(k == 0), stop=False)
                pe.matmul(tp[:, 0, 0:T], WGH[:, cols], AL[:, k], start=False, stop=False)
                mm = pe.matmul(tp[:, 0, 0:T], WGL[:, cols], AH[:, k], start=False, stop=(k == KT - 1))
            mm.then_inc(gate_pe, 1)
            pe.wait_ge(acc_free[0], A_OUT1)
            pe.wait_ge(acc_free[1], A_OUT1)
            pe.wait_ge(gate_v, 1)
            for hp in range(PAIRS):
                if hp >= 4:
                    pe.wait_ge((qk_copied, qk_copied_v)[hp % 2], (hp - 4) // 2 + 1)
                for m, col in enumerate((QA1, KA1)):
                    for tb in range(TB):
                        mm = pe.transpose(tp[:, hp % 4, m * T + tb * P:m * T + (tb + 1) * P],
                                          P1[:, tb, col + hp * P:col + (hp + 1) * P], ident[:])
                mm.then_inc(qk_turned, 1)
            pe.wait_ge(qk_copied, 4)
            pe.wait_ge(qk_copied_v, 4)

            def half(h):
                return slice((h % 2) * HD, (h % 2 + 1) * HD)

            softmax_attention(0, lambda h, a, b: QK[half(h), h // 2, 0, a:b], lambda h, a, b: QK[half(h), h // 2, 1, a:b],
                              lambda h, kb: P1[:, kb, VA1 + h * HD:VA1 + (h + 1) * HD], PB, PT)
            pe.wait_ge(gla_in, 32)
            pe.wait_ge(y_ready, 4)
            for tb in range(TB):
                mm = pe.matmul(acc_bank(tb), glT[:, tb * P:(tb + 1) * P], wgu[:], start=True, stop=True)
            mm.then_inc(gla_pe, 1)
            for h in range(GLA_HEADS):
                for m, col in enumerate((QG1, KG1)):
                    for tb in range(TB):
                        mm = pe.transpose(tp[:, h, m * T + tb * P:m * T + (tb + 1) * P],
                                          P1[:, tb, col + h * P:col + (h + 1) * P], ident[:])
            mm.then_inc(gla_pe, 1)
            pe.wait_ge(gla_v, GV_LA)
            for tb in range(TB):
                for h in range(GLA_HEADS):
                    mm = pe.matmul(acc_bank(2 + h // 2)[:, (h % 2) * T + tb * P:(h % 2) * T + (tb + 1) * P],
                                   LA[:, tb, h * P:(h + 1) * P], tri_le[:], start=True, stop=True)
            mm.then_inc(gla_pe, 1)
            for tb in range(TB):
                mm = pe.matmul(acc_bank(tb), tri_gt[:], LA[:, tb, :], start=True, stop=True)
            mm.then_inc(gla_pe, 1)
            pe.wait_ge(gla_v, GV_KE)
            for c in range(3):
                rows_c = slice((c % 2) * LOOK, (c % 2 + 1) * LOOK)
                if c == 2:
                    pe.wait_ge(gla_v, GV_ST1)
                for h in range(GLA_HEADS):
                    mm = pe.matmul(acc_bank(2 * (c % 2) + h // 2)[:, (h % 2) * GLA_DV:(h % 2 + 1) * GLA_DV],
                                   KE[rows_c, c // 2, h * P:(h + 1) * P],
                                   P1[rows_c, c // 2, VG1 + h * GLA_DV:VG1 + (h + 1) * GLA_DV], start=True, stop=True)
                mm.then_inc(gla_pe, 1)
            for tb in range(TB):
                for h in range(GLA_HEADS):
                    cols = slice(tb * P, (tb + 1) * P)
                    mm = pe.matmul(tp[:, tb, h * P:(h + 1) * P], KI[:, h, cols], QD[:, h, cols], start=True, stop=True)
            mm.then_inc(gla_pe, 1)
            pe.wait_ge(gla_p, 2)
            pe.wait_ge(gla_v, GV_ST2)
            for tb in range(TB):
                for h in range(GLA_HEADS):
                    o = acc_bank(2 * tb + h // 2)[:, (h % 2) * GLA_DV:(h % 2 + 1) * GLA_DV]
                    first = pe.matmul(o, AT[:, tb * GLA_HEADS + h, :],
                                      P1[:, tb, VG1 + h * GLA_DV:VG1 + (h + 1) * GLA_DV],
                                      start=(h % 2 == 0), stop=True, skip_group_check=True)
                    for half_ in range(2):
                        c = 2 * tb + half_
                        if c == 0:
                            continue
                        mm = pe.matmul(o[half_ * LOOK:(half_ + 1) * LOOK, :],
                                       QD[:, h, c * LOOK:(c + 1) * LOOK], ST[:, c - 1, h, :],
                                       start=False, stop=True, skip_group_check=True)
            mm.then_inc(gla_pe, 1)
            pe.wait_ge(gla_v, GV_END)

            def y1_cols(kt, tb):
                col = kt * P if kt < KT // 2 else RG1 + (kt - KT // 2) * P
                return P1[:, tb, col:col + P]

            turn(y1_cols, KT, G_Y1)
            two_tiles(ZH, ZL, C_OUT1, A_OUT1, 2, KT, groups=G_Y1)
            turn_x(slices_of(A_OUT1), G_F1)

            def turn_u(a, it, first):
                def go():
                    pe.wait_ge(acc_free[a], A_UP1 + it + 1)
                    if not first:
                        pe.wait_ge(h_lo, it)
                    for fb in range(4):
                        for tb in range(TB):
                            mm = pe.transpose(tp[:, 2 * a + fb // 2, (fb % 2) * T + tb * P:(fb % 2) * T + (tb + 1) * P],
                                              U[:, a, tb, fb * P:(fb + 1) * P], ident[:])
                        if fb % 2:
                            mm.then_inc(u_turned, 1)
                return go

            tile(AH, AL, KT, C_UP1, 0, 0, A_UP1, groups=G_F1)
            tile(AH, AL, KT, C_UP1, 8, 1, A_UP1, between=turn_u(0, 0, True))
            tile(AH, AL, KT, C_UP1, 16, 0, A_UP1 + 1, between=turn_u(1, 0, True))
            tile(AH, AL, KT, C_UP1, 24, 1, A_UP1 + 1, between=turn_u(0, 1, False))
            with pe.Fori(2, FF // NT) as i:
                tile(AH, AL, KT, C_UP1, 0, 0, A_UP1, i, 16, between=turn_u(1, i - 1, False))
                tile(AH, AL, KT, C_UP1, 8, 1, A_UP1, i, 16, between=turn_u(0, i, False))
            turn_u(1, FF // NT - 1, False)()
            pe.wait_ge(h_lo, FF // NT)
            two_tiles(BH, BL, C_DOWN1, A_DOWN1, 2, FKT)
            pe.wait_ge(p_in, 16)
            turn(lambda k, tb: pin[:, tb, k * P:(k + 1) * P], 2, G_P)
            for n in range(D // NT):
                tile(PTH, PTL, CHUNK_KT, C_PROJ, n, n % 2, A_PROJ + n // 2, groups=G_P)
            turn_x(slices_of(A_DOWN1), G_PLE)
            two_tiles(AH, AL, C_PLE, A_PLE, 2, KT, groups=G_PLE)
            turn_x(slices_scaled(X_NORM), G_X2)
            two_tiles(AH, AL, C_IN2, A_IN2, 8, KT, groups=G_X2)
            tile(AH, AL, KT, C_IN2, 128, 0, A_IN2 + 8)
            pe.wait_ge(acc_free[0], A_BR[0])
            pe.wait_ge(acc_free[1], A_BR[1])
            for hp in range(PAIRS // 2):
                for m in range(2):
                    for tb in range(TB):
                        mm = pe.transpose(tp[:, hp, m * T + tb * P:m * T + (tb + 1) * P],
                                          PQ[:, tb, QA2 + (2 * hp + m) * P:QA2 + (2 * hp + m + 1) * P], ident[:])
                mm.then_inc(qk_turned, 1)
            pe.wait_ge(kd_done, 7)
            for g in range(KV_HEADS // 2):
                for m in range(2):
                    for tb in range(TB):
                        mm = pe.transpose(acc_bank(g)[:, m * T + tb * P:m * T + (tb + 1) * P],
                                          KD[:, tb, 2 * g + m, :, :].rearrange("p a b -> p (a b)"), ident[:])
                mm.then_inc(qk_turned, 1)
            pe.wait_ge(qk_copied, 8)
            pe.wait_ge(qk_copied_v, 6)
            softmax_attention(HEADS, lambda h, a, b: QT2[half(h), h // 2, a:b],
                              lambda h, a, b: KT2[half(h), h // GROUP, a:b],
                              lambda h, kb: PQ[:, kb, VA2 + (h // GROUP) * HD:VA2 + (h // GROUP + 1) * HD], PB2, PT2)
            pe.wait_ge(y_ready, 8)
            for hp in range(PAIRS):
                if hp >= 4:
                    pe.wait_ge((qk_copied, qk_copied_v)[hp % 2], (8, 6)[hp % 2] + (hp - 4) // 2 + 1)
                for m, col in enumerate((QB2, KB2)):
                    for tb in range(TB):
                        mm = pe.transpose(tp[:, hp % 4, m * T + tb * P:m * T + (tb + 1) * P],
                                          PQ[:, tb, col + hp * P:col + (hp + 1) * P], ident[:])
                mm.then_inc(qk_turned, 1)
            pe.wait_ge(qk_copied, 12)
            pe.wait_ge(qk_copied_v, 10)
            for q in range(HEADS // 4):
                for i in range(4):
                    h = 4 * q + i
                    if q:
                        pe.wait_ge(a_done, h - 3)
                    z = tp[:, i, :]
                    pe.matmul(z[:, 0:T], QKB[half(h), h // 2, 1, 0:P], QKB[half(h), h // 2, 0, 0:T],
                              start=True, stop=False, skip_group_check=True)
                    pe.matmul(z[:, T:3 * P], QKB[half(h), h // 2, 1, P:T], QKB[half(h), h // 2, 0, P:T],
                              start=False, stop=False, skip_group_check=True)
                    pe.matmul(z[:, 0:P], ident[:], neg_mask[:], start=False, stop=False, skip_group_check=True)
                    pe.matmul(z[:, T:3 * P], ident[:], neg_mask[:], start=False, stop=True,
                              skip_group_check=True).then_inc(z_full, 1)
                for i in range(4):
                    h = 4 * q + i
                    pe.wait_ge(sp_done, h + 1)
                    z = tp[:, i, :]
                    pe.matmul(z[:, 0:T], neg_tri[:], SE[:, i, 0:T], start=False, stop=False, skip_group_check=True)
                    pe.matmul(z[:, T:3 * P], neg_tri[:], SE[:, i, T:3 * P], start=False, stop=False,
                              skip_group_check=True)
                    pe.matmul(z[:, P:T], neg_ones[:], SE[:, i, T:3 * P], start=False, stop=True,
                              skip_group_check=True).then_inc(arg_full, 1)
                for i in range(4):
                    h = 4 * q + i
                    pe.wait_ge(a_done, h + 1)
                    for qb in range(TB):
                        o = acc_bank(2 * qb + h // 8)[:, (h % 8) * HD:(h % 8 + 1) * HD]
                        for kb in range(qb + 1):
                            blk = qb + kb
                            mm = pe.matmul(o, SA[:, h % 2, blk * P:(blk + 1) * P],
                                           PQ[:, kb, VB2 + h * HD:VB2 + (h + 1) * HD], start=(kb == 0), stop=(kb == qb))
                    mm.then_inc(stick_pv, 1)
            pe.wait_ge(y_ready, 12)

            def y2_cols(kt, tb):
                col = QA2 + kt * P if kt < KT // 2 else QB2 + (kt - KT // 2) * P
                return PQ[:, tb, col:col + P]

            turn(y2_cols, KT, G_Y2)
            with pe.Fori(0, D // NT) as i:
                tile(AH, AL, KT // 2, C_BR, 0, 0, A_BR[0], i, 8, groups=G_Y2)
                tile(AH, AL, KT // 2, C_BR, 4, 1, A_BR[1], i, 8, kt0=KT // 2, groups=G_Y2)
            pe.wait_ge(m_ready, D // NT)
            turn(lambda kt, tb: PG[:, tb, kt * P:(kt + 1) * P], KT, G_M2)
            two_tiles(MH, ML, C_OUT2, A_OUT2, 2, KT, groups=G_M2)
            turn_x(slices_of(A_OUT2), G_F2)

            def turn_h(it, first):
                def go():
                    pe.wait_ge(acc_free[1], A_UP2[1] + it + 1)
                    if not first:
                        pe.wait_ge(hb_lo, 2 * it)
                    for fb in range(4):
                        for tb in range(TB):
                            mm = pe.transpose(tp[:, fb // 2, (fb % 2) * T + tb * P:(fb % 2) * T + (tb + 1) * P],
                                              HB[:, tb, fb * P:(fb + 1) * P], ident[:])
                        if fb % 2:
                            mm.then_inc(hb_turned, 1)
                return go

            tile(AH, AL, KT, C_UP2, 0, 0, A_UP2[0], groups=G_F2)
            tile(AH, AL, KT, C_UP2, 8, 1, A_UP2[1])
            tile(AH, AL, KT, C_UP2, 16, 0, A_UP2[0] + 1, between=turn_h(0, True))
            tile(AH, AL, KT, C_UP2, 24, 1, A_UP2[1] + 1)
            with pe.Fori(2, FF // NT) as i:
                tile(AH, AL, KT, C_UP2, 0, 0, A_UP2[0], i, 16, between=turn_h(i - 1, False))
                tile(AH, AL, KT, C_UP2, 8, 1, A_UP2[1], i, 16)
            turn_h(FF // NT - 1, False)()
            pe.wait_ge(hb_lo, 2 * (FF // NT))
            two_tiles(BH, BL, C_DOWN2, A_DOWN2, 2, FKT)

        @block.scalar
        def _(act):
            def hi(base, js, it=None, per=0):
                for j in js:
                    n = base + j
                    if n >= C_END:
                        continue
                    at = n if it is None else n + per * it
                    act.wait_ge(w_loaded[n % RING], 16 * (n // RING + 1) if it is None
                                else 16 * (n // RING + 1) + 16 * (per // RING) * it)
                    if it is not None or n >= RING:
                        act.wait_ge(chunk_used, at - RING + 1)
                    act.activation(WH[:, n % RING], WR[:, n % RING], ACT.Copy).then_inc(hi_done, 1)

            def turn(H, nkt, group, w=None):
                for g in range(nkt // 2):
                    n = group + g
                    act.wait_ge(turned, n + 1)
                    if w is None:
                        last = act.activation(H[:, 2 * g:2 * g + 2, :].rearrange("p a t -> p (a t)"), tp[:, n % 4, :],
                                              ACT.Copy)
                    else:
                        for k in range(2):
                            last = act.activation(H[:, 2 * g + k, :], tp[:, n % 4, k * T:(k + 1) * T], ACT.Copy,
                                                  scale=nw[:, w, 2 * g + k:2 * g + k + 1])
                    last.then_inc(turned_hi, 1)

            def squares(ready, norm):
                for n in range(4):
                    act.wait_ge(*ready(n))
                    if norm and n == 0:
                        act.wait_ge(sums, norm)
                    for tb in range(TB):
                        k = 8 * norm + 2 * n + tb
                        if k:
                            act.wait_ge(squared, k)
                        act.activation(junk[:], X[:, tb, n * NT:(n + 1) * NT], ACT.Square,
                                       accum_out=ss[:, tb, n:n + 1]).then_inc(squared, 1)

            def sqrt_of(norm):
                act.wait_ge(mean, norm + 1)
                act.activation(sroot[:], smean[:], ACT.Sqrt).then_inc(root, 1)

            def plain(base, n_it, per=16):
                with act.Fori(0, n_it) as i:
                    hi(base, range(4, 4 + per), i, per)

            for tb in range(TB):
                for n in range(4):
                    if tb + n == 0:
                        act.wait_ge(x_in, 16 * TB)
                    k = 4 * tb + n
                    if k:
                        act.wait_ge(squared, k)
                    act.activation(junk[:], X[:, tb, n * NT:(n + 1) * NT], ACT.Square,
                                   accum_out=ss[:, tb, n:n + 1]).then_inc(squared, 1)
            sqrt_of(N_IN1)
            act.wait_ge(vec_ready, 1)
            turn(AH, KT, G_X1, 0)
            hi(C_IN1, range(4))
            plain(C_IN1, 6)
            act.wait_ge(gate_in, 16)
            act.wait_ge(gate_pad, 1)
            act.activation(WGH[:, 0:KT * RANK], WG[:].rearrange("p k n -> p (k n)"), ACT.Copy).then_inc(gate_hi, 1)

            def copy_pairs(M, n0, count0):
                for hp in range(0, PAIRS, 2):
                    act.wait_ge(qk_turned, n0 + hp + 1)
                    act.activation(M[:, hp, 0, :], tp[:, hp % 4, 0:T], ACT.Copy, scale=HD ** -0.5)
                    act.activation(M[:, hp, 1, :], tp[:, hp % 4, T:2 * T], ACT.Copy).then_inc(qk_copied, 1)

            def exps(n, h, S, B, M, R):
                act.wait_ge(s_neg, n + 1)
                if n >= 2:
                    act.wait_ge(pt_full, n - 1)
                act.activation(B[:, n % 2, 0:P], S[:, n % 2, 0:P], ACT.Exp, bias=M[:, h, 0:1],
                               accum_out=R[:, h, 0:1])
                act.activation(B[:, n % 2, P:3 * P], S[:, n % 2, P:3 * P], ACT.Exp, bias=M[:, h, 1:2],
                               accum_out=R[:, h, 1:2]).then_inc(e_done, 1)

            def copy_weights(n, B):
                act.wait_ge(pt_full, n + 1)
                if n >= 2:
                    act.wait_ge(pv_done, n - 1)
                act.activation(B[:, n % 2, :], tp[:, 2 + n % 2, 0:3 * P], ACT.Copy).then_inc(pt_copied, 1)

            copy_pairs(QK, 0, 0)
            exps(0, 0, SB, PB, nmax, rsum)
            for h in range(HEADS):
                if h + 1 < HEADS:
                    exps(h + 1, h + 1, SB, PB, nmax, rsum)
                copy_weights(h, PT)
            act.wait_ge(gla_v, GV_NEG)
            act.activation(LE[:], LE[:], ACT.Exp).then_inc(gla_a, 1)
            act.wait_ge(gla_a, 1)
            act.activation(LE[:], LE[:], ACT.Ln, bias=1.0).then_inc(gla_a, 1)
            act.wait_ge(gla_pe, 3)
            for h in range(0, GLA_HEADS, 2):
                b = acc_bank(2 + h // 2)
                act.activation(EB[:, h:h + 2, :].rearrange("p a t -> p (a t)"), b, ACT.Exp)
                last = act.activation(EN[:, h:h + 2, :].rearrange("p a t -> p (a t)"), b, ACT.Exp, scale=-1.0)
            last.then_inc(gla_a, 1)
            act.wait_ge(gla_pe, 4)
            for tb in range(TB):
                last = act.activation(KE[:, tb, :], acc_bank(tb), ACT.Exp)
            last.then_inc(gla_a, 1)
            act.wait_ge(gla_pe, 8)
            act.wait_ge(gla_p, 1)
            for half_ in range(2):
                part = slice(half_ * LOOK, (half_ + 1) * LOOK)
                for tb in range(TB):
                    last = act.activation(AT[part, tb * GLA_HEADS:(tb + 1) * GLA_HEADS, part],
                                          tp[part, tb, :].rearrange("p (h t) -> p h t", h=GLA_HEADS)[:, :, part],
                                          ACT.Copy)
            last.then_inc(gla_a, 1)
            act.wait_ge(gla_pe, 9)
            act.wait_ge(squared, 8)
            n = 0
            for tb in range(TB):
                for h in range(GLA_HEADS):
                    act.wait_ge(gla_a, 5 + n)
                    act.activation(junk[:, 0:GLA_DV], acc_bank(2 * tb + h // 2)[:, (h % 2) * GLA_DV:(h % 2 + 1) * GLA_DV],
                                   ACT.Square, accum_out=osq[:, tb, h:h + 1]).then_inc(gla_a, 1)
                    n += 1
            act.activation(SR[:], P1[:, :, RG1:RG1 + GLA_W], ACT.Silu).then_inc(gla_a, 1)
            act.wait_ge(gla_v, GV_OSM)
            act.activation(osr[:], osm[:], ACT.Sqrt).then_inc(gla_a, 1)
            turn(ZH, KT, G_Y1)
            plain(C_OUT1, 2)
            squares(slices_of(A_OUT1), N_F1)
            sqrt_of(N_F1)
            turn(AH, KT, G_F1, 1)
            def evac_u(a, it):
                act.wait_ge(chunk_used, C_UP1 + 8 * (a + 1) + 16 * it)
                act.activation(U[:, a, 0, :], acc[:, a, 0, :], ACT.Copy, scale=inv[:, N_F1, 0:1])
                act.activation(U[:, a, 1, :], acc[:, a, 1, :], ACT.Copy, scale=inv[:, N_F1, 1:2]).then_inc(acc_free[a], 1)

            def start_conv(a, b, it):
                act.wait_ge(u_turned, 4 * it + 2 * a + b + 1)
                for k in range(2):
                    fb = 2 * b + k
                    f = it * 4 + (a * FKT + fb)
                    last = act.activation(CV[:, a, fb, :], tp[:, 2 * a + b, k * T:(k + 1) * T], ACT.Identity,
                                          bias=cw[:, 3, bass.ds(f, 1)], scale=cw[:, 2, bass.ds(f, 1)])
                last.then_inc(c_init, 1)

            def up1(it, split, i, last):
                split(range(8, 12))
                evac_u(0, it)
                split(range(12, 14))
                start_conv(0, 0, it)
                split(range(14, 15))
                start_conv(0, 1, it)
                split(range(15, 17))
                act.wait_ge(conv_done, 4 * it + 2)
                act.activation(CV[:, 0], CV[:, 0], ACT.Gelu_apprx_tanh).then_inc(gelu_done, 1)
                split(range(17, 20))
                evac_u(1, it)
                if not last:
                    split(range(20, 22))
                start_conv(1, 0, it)
                if not last:
                    split(range(22, 23))
                start_conv(1, 1, it)
                if not last:
                    split(range(23, 24))
                act.wait_ge(h_ready, it + 1)
                act.activation(BH[:, bass.ds(it * 4, 4), :], CV[:, 0], ACT.Copy).then_inc(h_hi, 1)

            hi(C_UP1, range(4, 8))
            with act.Fori(0, FF // NT - 1) as i:
                up1(i, lambda js: hi(C_UP1, js, i, 16), i, False)
            n = FF // NT - 1
            up1(n, lambda js: hi(C_UP1 + 16 * n, js), n, True)
            plain(C_DOWN1, 2, FKT)
            turn(PTH, 2, G_P)
            hi(C_PROJ, range(4, 8))
            squares(slices_of(A_DOWN1), N_PLE)
            sqrt_of(N_PLE)
            turn(AH, KT, G_PLE, 2)

            def gate(a, it, first=False):
                act.wait_ge(chunk_used, C_PLE + 8 * (a + 1) + 16 * it)
                if not first:
                    act.wait_ge(x_scaled, X_PLE + 2 * it + a)
                for tb in range(TB):
                    last = act.activation(GT[:, tb, :], acc[:, a, tb, :], ACT.Sigmoid, scale=inv[:, N_PLE, tb:tb + 1])
                last.then_inc(acc_free[a], 1)

            for n in range(D // NT):
                hi(C_PLE + 8 * n, range(4, 12))
                gate(n % 2, n // 2, first=(n == 0))
            squares(slices_scaled(X_PLE), N_END1)
            sqrt_of(N_END1)
            squares(slices_scaled(X_NORM), N_IN2)
            sqrt_of(N_IN2)
            turn(AH, KT, G_X2, 3)
            plain(C_IN2, 8)
            hi(C_IN2 + 128, range(4, 12))
            for hp in range(PAIRS // 2):
                act.wait_ge(qk_turned, PAIRS + hp + 1)
                act.activation(QT2[:, 2 * hp:2 * hp + 2, :].rearrange("p a t -> p (a t)"), tp[:, hp, :], ACT.Copy,
                               scale=HD ** -0.5).then_inc(qk_copied, 1)
            exps(HEADS, 0, SB2, PB2, nmax2, rsum2)
            for h in range(HEADS):
                if h + 1 < HEADS:
                    exps(HEADS + h + 1, h + 1, SB2, PB2, nmax2, rsum2)
                copy_weights(HEADS + h, PT2)
            act.wait_ge(sink_v, 1)
            act.activation(sk2[:], sk2[:], ACT.Exp).then_inc(sink_a, 1)
            copy_pairs(QKB, PAIRS + 6, 0)
            for q in range(HEADS // 4):
                for i in range(4):
                    act.wait_ge(z_read, 4 * q + i + 1)
                    act.activation(SE[:, i, :], SE[:, i, :], ACT.Exp).then_inc(ez_done, 1)
                for i in range(4):
                    act.wait_ge(ez_done, 4 * q + i + 1)
                    act.activation(SE[:, i, :], SE[:, i, :], ACT.Ln, bias=1.0).then_inc(ln_done, 1)
                for i in range(4):
                    h = 4 * q + i
                    act.wait_ge(arg_full, h + 1)
                    if h >= 2:
                        act.wait_ge(stick_pv, h - 1)
                    act.activation(SA[:, h % 2, :], tp[:, i, 0:3 * P], ACT.Exp).then_inc(a_done, 1)
            for half_ in range(2):
                act.activation(PG[:, :, half_ * D:(half_ + 1) * D], PG[:, :, half_ * D:(half_ + 1) * D],
                               ACT.Sigmoid).then_inc(sg_done, 1)
            turn(AH, KT, G_Y2)
            with act.Fori(0, D // NT) as i:
                hi(C_BR, range(4, 12), i, 8)
            turn(MH, KT, G_M2)
            plain(C_OUT2, 2)
            squares(slices_of(A_OUT2), N_F2)
            sqrt_of(N_F2)
            turn(AH, KT, G_F2, 4)

            def up2(it, split, last):
                split(range(8, 12))
                act.wait_ge(chunk_used, C_UP2 + 8 + 16 * it)
                for tb in range(TB):
                    s = act.activation(SG[:, tb, :], acc[:, 0, tb, :], ACT.Silu, scale=inv[:, N_F2, tb:tb + 1])
                s.then_inc(acc_free[0], 1)
                split(range(12, 20))
                if not last:
                    split(range(20, 22))
                for b in range(2):
                    act.wait_ge(hb_turned, 2 * it + b + 1)
                    act.activation(BH[:, bass.ds(it * 4 + 2 * b, 2), :].rearrange("p a t -> p (a t)"), tp[:, b, :],
                                   ACT.Copy).then_inc(hb_hi, 1)
                if not last:
                    split(range(22, 24))

            hi(C_UP2, range(4, 8))
            with act.Fori(0, FF // NT - 1) as i:
                up2(i, lambda js: hi(C_UP2, js, i, 16), False)
            n2 = FF // NT - 1
            up2(n2, lambda js: hi(C_UP2 + 16 * n2, js), True)
            hi(C_DOWN2, range(4, 2 * FKT))
            squares(slices_of(A_DOWN2), N_END2)
            sqrt_of(N_END2)

        @block.vector
        def _(dve):
            def lo(base, js, it=None, per=0):
                for j in js:
                    n = base + j
                    if n >= C_END:
                        continue
                    at = n if it is None else n + per * it
                    dve.wait_ge(hi_done, at + 1)
                    dve.tensor_tensor(WL[:, n % RING], WR[:, n % RING], WH[:, n % RING].bitcast(F32),
                                      ALU.subtract).then_inc(lo_done, 1)

            def turn(H, L, nkt, group, w=None):
                for g in range(nkt // 2):
                    n = group + g
                    dve.wait_ge(turned_hi, n + 1)
                    if w is None:
                        last = dve.tensor_tensor(L[:, 2 * g:2 * g + 2, :].rearrange("p a t -> p (a t)"), tp[:, n % 4, :],
                                                 H[:, 2 * g:2 * g + 2, :].bitcast(F32).rearrange("p a t -> p (a t)"),
                                                 ALU.subtract)
                    else:
                        for k in range(2):
                            last = dve.scalar_tensor_tensor(
                                L[:, 2 * g + k, :], tp[:, n % 4, k * T:(k + 1) * T], nw[:, w, 2 * g + k:2 * g + k + 1],
                                H[:, 2 * g + k, :].bitcast(F32), ALU.mult, ALU.subtract)
                    last.then_inc(turned_lo, 1)

            def norm(n):
                dve.wait_ge(squared, 8 * (n + 1))
                dve.tensor_reduce(ssum[:], ss[:], AXX, ALU.add).then_inc(sums, 1)
                dve.wait_ge(sums, n + 1)
                dve.tensor_scalar(smean[:], ssum[:], 1.0 / D, EPS, ALU.mult, ALU.add).then_inc(mean, 1)
                dve.wait_ge(root, n + 1)
                dve.reciprocal(inv[:, n, :], sroot[:]).then_inc(inv_ready, 1)
                dve.wait_ge(inv_ready, n + 1)

            def scaled(dst, a, base, it, n):
                dve.wait_ge(chunk_used, base + 8 * (a + 1) + 16 * it)
                for tb in range(TB):
                    last = dve.tensor_scalar(dst(tb), acc[:, a, tb, :], inv[:, n, tb:tb + 1], None, ALU.mult)
                last.then_inc(acc_free[a], 1)

            def residual(n, a, end, it=0, per=0):
                dve.wait_ge(chunk_used, end + per * it)
                for tb in range(TB):
                    xs = X[:, tb, bass.ds(n * NT, NT)]
                    last = dve.tensor_tensor(xs, acc[:, a, tb, :], xs, ALU.add)
                last.then_inc(acc_free[a], 1)

            def two_residuals(base, per):
                with dve.Fori(0, 2) as i:
                    lo(base, range(4, 4 + per // 2), i, per)
                    residual(2 * i, 0, base + per // 2, i, per)
                    lo(base, range(4 + per // 2, 4 + per), i, per)
                    residual(2 * i + 1, 1, base + per, i, per)

            dve.memset(nmax[:, 0, 0:1], 0.0).then_inc(acc_free[0], 1)
            dve.memset(nmax[:, 0, 1:2], 0.0).then_inc(acc_free[1], 1)
            dve.wait_ge(vec_turned, 1)
            dve.tensor_copy(vec[:], acc_bank(3)[:, 0:5 * KT + 8 * FKT]).then_inc(vec_ready, 1)
            norm(N_IN1)
            turn(AH, AL, KT, G_X1, 0)
            lo(C_IN1, range(4))
            dve.memset(WGH[:, KT * RANK:].bitcast(F32), 0.0)
            dve.memset(WGL[:, KT * RANK:].bitcast(F32), 0.0).then_inc(gate_pad, 1)
            with dve.Fori(0, 6) as i:
                lo(C_IN1, range(4, 12), i, 16)
                scaled(lambda tb: P1[:, tb, bass.ds(i * (2 * NT), NT)], 0, C_IN1, i, N_IN1)
                lo(C_IN1, range(12, 20), i, 16)
                scaled(lambda tb: P1[:, tb, bass.ds(i * (2 * NT) + NT, NT)], 1, C_IN1, i, N_IN1)
            dve.wait_ge(gate_hi, 1)
            dve.tensor_tensor(WGL[:, 0:KT * RANK], WG[:].rearrange("p k n -> p (k n)"),
                              WGH[:, 0:KT * RANK].bitcast(F32), ALU.subtract).then_inc(gate_lo, 1)
            dve.wait_ge(gate_pe, 1)
            dve.tensor_copy(glT[:], tp[0:RANK, 0, 0:T]).then_inc(gate_v, 1)

            def copy_pairs(M, n0):
                for hp in range(1, PAIRS, 2):
                    dve.wait_ge(qk_turned, n0 + hp + 1)
                    dve.tensor_scalar(M[:, hp, 0, :], tp[:, hp % 4, 0:T], HD ** -0.5, None, ALU.mult)
                    dve.tensor_copy(M[:, hp, 1, :], tp[:, hp % 4, T:2 * T]).then_inc(qk_copied_v, 1)

            def maxima(n, h, S, add_bias, R, M):
                dve.wait_ge(s_full, n + 1)
                if n >= 2:
                    dve.wait_ge(e_done, n - 1)
                add_bias(h, S[:, n % 2, :], tp[:, n % 2, :]).then_inc(s_read, 1)
                dve.wait_ge(s_read, n + 1)
                dve.tensor_reduce(R[:, h, 0:1], S[:, n % 2, 0:P], AXX, ALU.max)
                dve.tensor_reduce(R[:, h, 1:2], S[:, n % 2, P:3 * P], AXX, ALU.max).then_inc(s_max, 1)
                dve.wait_ge(s_max, n + 1)
                dve.tensor_scalar(M[:, h, :], R[:, h, :], -1.0, None, ALU.mult).then_inc(s_neg, 1)

            def band_bias(h, s, z):
                dve.tensor_tensor(s[:, 0:P], z[:, 0:P], BIAS[:, h, 2 * P - 1:P - 1:-1], ALU.add)
                return dve.tensor_tensor(s[:, P:3 * P], z[:, P:3 * P], BIAS[:, h, 3 * P - 1:P - 1:-1], ALU.add)

            def finish(R, C, dst, count):
                for qb in range(TB):
                    for g in range(2):
                        o = acc_bank(2 * qb + g).rearrange("p (h d) -> p h d", d=HD)
                        y = dst(qb, g).rearrange("p (h d) -> p h d", d=HD)
                        if C is None:
                            last = dve.tensor_copy(y, o)
                        else:
                            last = dve.tensor_tensor(y, o, wide(C[:, 8 * g:8 * g + 8, qb:qb + 1], [P, 8, HD]), ALU.mult)
                        last.then_inc(y_ready, 1)

            copy_pairs(QK, 0)
            dve.wait_ge(bias_masked, 1)
            for h in range(HEADS):
                maxima(h, h, SB, band_bias, rmax, nmax)
            dve.wait_ge(e_done, HEADS)
            dve.reciprocal(rrec[:], rsum[:]).then_inc(rec_done, 1)
            dve.wait_ge(rec_done, 1)
            dve.wait_ge(pv_done, HEADS)
            finish(rsum, rrec, lambda qb, g: P1[:, qb, QA1 + g * NT:QA1 + (g + 1) * NT], 0)

            gv = [0]

            def step(ins):
                gv[0] += 1
                ins.then_inc(gla_v, 1)
                dve.wait_ge(gla_v, gv[0])

            dve.wait_ge(gla_in, 32)
            dve.wait_ge(gla_pe, 1)
            for tb in range(TB):
                step(dve.scalar_tensor_tensor(LG[:, tb, :], acc_bank(tb), inv[:, N_IN1, tb:tb + 1], bgb[:],
                                              ALU.mult, ALU.add))
            step(dve.tensor_scalar(LA[:], LG[:], 0.0, None, ALU.min))
            step(dve.scalar_tensor_tensor(LE[:].rearrange("p a n -> p (a n)"), LA[:].rearrange("p a n -> p (a n)"), 2.0,
                                          LG[:].rearrange("p a n -> p (a n)"), ALU.mult, ALU.subtract))
            assert gv[0] == GV_NEG
            dve.wait_ge(gla_a, 2)
            step(dve.tensor_tensor(LA[:], LA[:], LE[:], ALU.subtract))
            step(dve.tensor_scalar(LA[:], LA[:], 1.0 / TAU, None, ALU.mult))
            assert gv[0] == GV_LA
            dve.wait_ge(gla_a, 3)
            for h in range(GLA_HEADS):
                step(dve.scalar_tensor_tensor(QD[:, h, :], tp[:, h, 0:T], GLA_DK ** -0.5, EB[:, h, :], ALU.mult, ALU.mult))
                step(dve.tensor_tensor(KI[:, h, :], tp[:, h, T:2 * T], EN[:, h, :], ALU.mult))
            dve.wait_ge(gla_a, 4)
            step(dve.tensor_tensor(KE[:], KE[:], P1[:, :, KG1:KG1 + GLA_KW], ALU.mult))
            assert gv[0] == GV_KE
            for c in range(3):
                dve.wait_ge(gla_pe, 5 + c)
                for h in range(GLA_HEADS):
                    upd = acc_bank(2 * (c % 2) + h // 2)[:, (h % 2) * GLA_DV:(h % 2 + 1) * GLA_DV]
                    if c == 0:
                        step(dve.tensor_copy(ST[:, 0, h, :], upd))
                    else:
                        step(dve.scalar_tensor_tensor(ST[:, c, h, :], ST[:, c - 1, h, :],
                                                      EB[:, h, (c + 1) * LOOK - 1:(c + 1) * LOOK], upd,
                                                      ALU.mult, ALU.add))
                if c == 0:
                    assert gv[0] == GV_ST1
            assert gv[0] == GV_ST2
            dve.wait_ge(gla_a, 13)
            step(dve.tensor_scalar(osm[:], osq[:], 1.0 / GLA_DV, EPS, ALU.mult, ALU.add))
            assert gv[0] == GV_OSM
            dve.wait_ge(gla_a, 15)
            step(dve.reciprocal(oiv[:], osr[:]))
            dve.wait_ge(gla_in, 48)
            for tb in range(TB):
                step(dve.tensor_tensor(SR[:, tb, :].rearrange("p (h d) -> p h d", d=GLA_DV),
                                       SR[:, tb, :].rearrange("p (h d) -> p h d", d=GLA_DV),
                                       wide(gnw[:, None, :], [P, GLA_HEADS, GLA_DV]), ALU.mult))
                for h in range(GLA_HEADS):
                    cols = slice(h * GLA_DV, (h + 1) * GLA_DV)
                    step(dve.scalar_tensor_tensor(P1[:, tb, RG1 + h * GLA_DV:RG1 + (h + 1) * GLA_DV],
                                                  acc_bank(2 * tb + h // 2)[:, (h % 2) * GLA_DV:(h % 2 + 1) * GLA_DV],
                                                  oiv[:, tb, h:h + 1], SR[:, tb, cols], ALU.mult, ALU.mult))
            assert gv[0] == GV_END
            turn(ZH, ZL, KT, G_Y1)
            two_residuals(C_OUT1, 16)
            norm(N_F1)
            turn(AH, AL, KT, G_F1, 1)

            def taps(a, b, it):
                dve.wait_ge(c_init, 4 * it + 2 * a + b + 1)
                for tap, back in ((1, 1), (0, 2)):
                    if back == 2:
                        dve.wait_ge(tap1, 4 * it + 2 * a + b + 1)
                    for k in range(2):
                        fb = 2 * b + k
                        f = it * 4 + (a * FKT + fb)
                        last = dve.scalar_tensor_tensor(CV[:, a, fb, back:T], tp[:, 2 * a + b, k * T:(k + 1) * T - back],
                                                        cw[:, tap, bass.ds(f, 1)], CV[:, a, fb, back:T],
                                                        ALU.mult, ALU.add)
                    last.then_inc(tap1 if back == 1 else conv_done, 1)

            def up1(it, split, last):
                split(range(8, 14))
                taps(0, 0, it)
                split(range(14, 15))
                taps(0, 1, it)
                split(range(15, 20))
                if not last:
                    split(range(20, 22))
                taps(1, 0, it)
                if not last:
                    split(range(22, 23))
                taps(1, 1, it)
                if not last:
                    split(range(23, 24))
                dve.wait_ge(gelu_done, it + 1)
                dve.wait_ge(conv_done, 4 * it + 4)
                dve.tensor_tensor(CV[:, 0], CV[:, 0], CV[:, 1], ALU.mult).then_inc(h_ready, 1)
                dve.wait_ge(h_hi, it + 1)
                dve.tensor_tensor(BL[:, bass.ds(it * 4, 4), :], CV[:, 0], BH[:, bass.ds(it * 4, 4), :].bitcast(F32),
                                  ALU.subtract).then_inc(h_lo, 1)

            lo(C_UP1, range(4, 8))
            with dve.Fori(0, FF // NT - 1) as i:
                up1(i, lambda js: lo(C_UP1, js, i, 16), False)
            n = FF // NT - 1
            up1(n, lambda js: lo(C_UP1 + 16 * n, js), True)
            two_residuals(C_DOWN1, FKT)
            turn(PTH, PTL, 2, G_P)
            for n in range(D // NT):
                dve.wait_ge(chunk_used, C_PROJ + n + 1)
                for tb in range(TB):
                    last = dve.tensor_copy(PP[:, tb, n * NT:(n + 1) * NT], acc[:, n % 2, tb, :])
                last.then_inc(acc_free[n % 2], 1)
                lo(C_PROJ, [4 + n])
            norm(N_PLE)
            turn(AH, AL, KT, G_PLE, 2)

            def gated(n):
                dve.wait_ge(acc_free[n % 2], A_PLE + n // 2 + 1)
                cols = slice(n * NT, (n + 1) * NT)
                dve.tensor_tensor(GT[:], GT[:], PP[:, :, cols], ALU.mult).then_inc(g_mul, 1)
                dve.wait_ge(g_mul, n + 1)
                dve.tensor_tensor(X[:, :, cols], X[:, :, cols], GT[:], ALU.add).then_inc(x_scaled, 1)

            for n in range(D // NT):
                lo(C_PLE + 8 * n, range(4, 12))
                gated(n)
            norm(N_END1)
            dve.wait_ge(fw_in, 16)
            for n in range(D // NT):
                cols = slice(n * NT, (n + 1) * NT)
                for tb in range(TB):
                    last = dve.scalar_tensor_tensor(X[:, tb, cols], X[:, tb, cols], inv[:, N_END1, tb:tb + 1],
                                                    fw[:, cols], ALU.mult, ALU.mult)
                last.then_inc(x_scaled, 1)
            norm(N_IN2)
            turn(AH, AL, KT, G_X2, 3)
            def to_pq(n):
                return lambda tb: PQ[:, tb, bass.ds(n * NT, NT)]

            def to_pg(n):
                return lambda tb: PG[:, tb, bass.ds(n * NT, NT)]

            with dve.Fori(0, 4) as i:
                lo(C_IN2, range(4, 12), i, 16)
                scaled(to_pq(2 * i), 0, C_IN2, i, N_IN2)
                lo(C_IN2, range(12, 20), i, 16)
                scaled(to_pq(2 * i + 1), 1, C_IN2, i, N_IN2)
            lo(C_IN2 + 64, range(4, 12))
            scaled(to_pq(8), 0, C_IN2, 4, N_IN2)
            lo(C_IN2 + 64, range(12, 20))
            scaled(to_pg(0), 1, C_IN2, 4, N_IN2)
            with dve.Fori(5, 8) as i:
                lo(C_IN2, range(4, 12), i, 16)
                scaled(to_pg(2 * i - 9), 0, C_IN2, i, N_IN2)
                lo(C_IN2, range(12, 20), i, 16)
                scaled(to_pg(2 * i - 8), 1, C_IN2, i, N_IN2)
            lo(C_IN2 + 128, range(4, 12))
            scaled(to_pg(7), 0, C_IN2, 8, N_IN2)
            for g in range(2):
                dve.wait_ge(qk_turned, PAIRS + 4 + g + 1)
                dve.tensor_copy(KT2[:, 2 * g:2 * g + 2, :].rearrange("p a t -> p (a t)"),
                                acc_bank(g)).then_inc(qk_copied_v, 1)

            def window_bias(h, s, z):
                slope = -(2.0 ** (-8.0 * (h + 1) / HEADS))
                dve.scalar_tensor_tensor(s[:, 0:P], dist[:, P:2 * P], slope, z[:, 0:P], ALU.mult, ALU.add)
                return dve.scalar_tensor_tensor(s[:, P:3 * P], dist[:], slope, z[:, P:3 * P], ALU.mult, ALU.add)

            dve.wait_ge(sk_in, 16)
            dve.wait_ge(kd_done, 3)
            for h in range(HEADS):
                n = HEADS + h
                dve.wait_ge(s_full, n + 1)
                dve.wait_ge(e_done, n - 1)
                window_bias(h, SB2[:, n % 2, :], tp[:, n % 2, :]).then_inc(s_read, 1)
                dve.wait_ge(s_read, n + 1)
                dve.tensor_reduce(rmax2[:, h, 0:1], SB2[:, n % 2, 0:P], AXX, ALU.max)
                dve.tensor_reduce(rmax2[:, h, 1:2], SB2[:, n % 2, P:3 * P], AXX, ALU.max).then_inc(s_max, 1)
                dve.wait_ge(s_max, n + 1)
                dve.tensor_scalar(nmax2[:, h, :], rmax2[:, h, :], sk[:, h:h + 1], -1.0, ALU.max,
                                  ALU.mult).then_inc(s_neg, 1)
            dve.wait_ge(s_neg, 2 * HEADS)
            dve.wait_ge(e_done, 2 * HEADS)
            dve.tensor_tensor(sk2[:], nmax2[:], wide(sk[:, :, None], [P, HEADS, 2]), ALU.add).then_inc(sink_v, 1)
            dve.wait_ge(sink_a, 1)
            dve.tensor_tensor(rsum2[:], rsum2[:], sk2[:], ALU.add).then_inc(sink_v, 1)
            dve.wait_ge(sink_v, 2)
            dve.reciprocal(rrec2[:], rsum2[:]).then_inc(rec_done, 1)
            dve.wait_ge(rec_done, 2)
            dve.wait_ge(pv_done, 2 * HEADS)
            finish(rsum2, rrec2, lambda qb, g: PQ[:, qb, QA2 + g * NT:QA2 + (g + 1) * NT], 4)
            copy_pairs(QKB, PAIRS + 6)
            for q in range(HEADS // 4):
                for i in range(4):
                    h = 4 * q + i
                    z = tp[:, i, 0:3 * P]
                    dve.wait_ge(z_full, h + 1)
                    dve.tensor_scalar(SM[:, i, :], z, 0.0, None, ALU.max).then_inc(m_done, 1)
                    dve.wait_ge(m_done, h + 1)
                    dve.scalar_tensor_tensor(SE[:, i, :], SM[:, i, :], -2.0, z, ALU.mult, ALU.add).then_inc(z_read, 1)
                for i in range(4):
                    h = 4 * q + i
                    dve.wait_ge(ln_done, h + 1)
                    dve.tensor_tensor(SE[:, i, :], SE[:, i, :], SM[:, i, :], ALU.add).then_inc(sp_done, 1)
            dve.wait_ge(stick_pv, HEADS)
            finish(None, None, lambda qb, g: PQ[:, qb, QB2 + g * NT:QB2 + (g + 1) * NT], 8)
            turn(AH, AL, KT, G_Y2)
            dve.wait_ge(sg_done, 2)

            with dve.Fori(0, D // NT) as i:
                lo(C_BR, range(4, 8), i, 8)
                ga, gb = PG[:, :, bass.ds(i * NT, NT)], PG[:, :, bass.ds(i * NT + D, NT)]
                dve.wait_ge(chunk_used, C_BR + 4 + 8 * i)
                dve.tensor_tensor(ga, acc[:, 0], ga, ALU.mult).then_inc(acc_free[0], 1)
                lo(C_BR, range(8, 12), i, 8)
                dve.wait_ge(chunk_used, C_BR + 8 + 8 * i)
                dve.tensor_tensor(gb, acc[:, 1], gb, ALU.mult).then_inc(acc_free[1], 1)
                dve.wait_ge(acc_free[0], A_BR[0] + i + 1)
                dve.wait_ge(acc_free[1], A_BR[1] + i + 1)
                dve.tensor_tensor(ga, ga, gb, ALU.add).then_inc(m_ready, 1)
            turn(MH, ML, KT, G_M2)
            two_residuals(C_OUT2, 16)
            norm(N_F2)
            turn(AH, AL, KT, G_F2, 4)

            def up2(it, split, last):
                split(range(8, 20))
                dve.wait_ge(chunk_used, C_UP2 + 16 + 16 * it)
                dve.wait_ge(acc_free[0], A_UP2[0] + it + 1)
                for tb in range(TB):
                    s = dve.scalar_tensor_tensor(HB[:, tb, :], acc[:, 1, tb, :], inv[:, N_F2, tb:tb + 1], SG[:, tb, :],
                                                 ALU.mult, ALU.mult)
                s.then_inc(acc_free[1], 1)
                if not last:
                    split(range(20, 22))
                for b in range(2):
                    dve.wait_ge(hb_hi, 2 * it + b + 1)
                    cols = bass.ds(it * 4 + 2 * b, 2)
                    dve.tensor_tensor(BL[:, cols, :].rearrange("p a t -> p (a t)"), tp[:, b, :],
                                      BH[:, cols, :].bitcast(F32).rearrange("p a t -> p (a t)"),
                                      ALU.subtract).then_inc(hb_lo, 1)
                if not last:
                    split(range(22, 24))

            lo(C_UP2, range(4, 8))
            with dve.Fori(0, FF // NT - 1) as i:
                up2(i, lambda js: lo(C_UP2, js, i, 16), False)
            n2 = FF // NT - 1
            up2(n2, lambda js: lo(C_UP2 + 16 * n2, js), True)
            for n in range(D // NT):
                lo(C_DOWN2 + n * (FKT // 2), range(4, 4 + FKT // 2))
                residual(n, n % 2, C_DOWN2 + (n + 1) * (FKT // 2))
            norm(N_END2)
            dve.wait_ge(fg_in, 16)
            for n in range(D // NT):
                cols = slice(n * NT, (n + 1) * NT)
                for tb in range(TB):
                    last = dve.scalar_tensor_tensor(X[:, tb, cols], X[:, tb, cols], inv[:, N_END2, tb:tb + 1],
                                                    fw2[:, cols], ALU.mult, ALU.mult)
                last.then_inc(x_scaled, 1)


_NAMES = ['x', 'p', 'norm_mix_w', 'w_in', 'att_rel_bias', 'w_gla_gate_up', 'b_gla_gate', 'gla_norm_w', 'w_out',
          'norm_ffn_w', 'w_ffn_up', 'w_ffn_conv', 'b_ffn_conv', 'w_ffn_down', 'norm_ple_w', 'w_ple_gate',
          'w_ple_proj', 'final_norm_w', 'norm_mix_g_2', 'w_in_2', 'sink_logits_2', 'w_branch_a_2', 'w_branch_b_2',
          'w_out_2', 'norm_ffn_g_2', 'w_ffn_in_2', 'w_ffn_down_2', 'norm_final_g_2']


def kernel(**inputs):
    import numpy as _np
    import concourse.bacc as _bacc
    from concourse import mybir as _mybir
    from concourse.bass_utils import run_bass_kernel_spmd as _run

    nc = _bacc.Bacc("TRN2", target_bir_lowering=False, num_devices=1)
    arrays, args = {}, []
    for name in _NAMES:
        a = _np.ascontiguousarray(inputs[name])
        while a.ndim > 1 and a.shape[0] == 1:
            a = a[0]
        arrays[f"in_{name}_dram"] = a
        args.append(nc.dram_tensor(f"in_{name}_dram", a.shape, _mybir.dt.from_np(a.dtype), kind="ExternalInput").ap())
    args.append(nc.dram_tensor("out_0_dram", (T, D), F32, kind="ExternalOutput").ap())
    two_blocks_kernel(nc, *args)
    r = _run(nc, [arrays], core_ids=[0])
    return r.results[0]["out_0_dram"].reshape(1, T, D)
```

```python
from contextlib import ExitStack

import concourse.bass as bass
from concourse import mybir


F32 = mybir.dt.float32
F32R = mybir.dt.float32r
ACT = mybir.ActivationFunctionType
ALU = mybir.AluOpType
AXX = mybir.AxisListType.X

P = 128
T = 256
TB = T // P
D = 2048
KT = D // P
NT = 512
EPS = 1e-6
RING = 4
CHUNK_KT = 2

HD = 64
HEADS = 16
PAIRS = HEADS // 2
MAX_REL = 256
ATT_W = HEADS * HD
GLA_HEADS = 4
GLA_DK = 128
GLA_DV = 256
GLA_KW = GLA_HEADS * GLA_DK
GLA_W = GLA_HEADS * GLA_DV
RANK = 16
TAU = 16.0
LOOK = 64
QA1, KA1, VA1 = 0, ATT_W, 2 * ATT_W
QG1 = 3 * ATT_W
KG1 = QG1 + GLA_KW
VG1 = KG1 + GLA_KW
RG1 = VG1 + GLA_W
GATE1 = RG1 + GLA_W
FF = 5632
FKT = FF // P

KV_HEADS = 4
GROUP = HEADS // KV_HEADS
WINDOW = P
QA2, KA2, VA2 = 0, 1024, 1280
QB2, KB2, VB2 = 1536, 2560, 3584
GATES2 = 4608

C_IN1 = 0
C_OUT1 = C_IN1 + GATE1 // NT * 8
C_UP1 = C_OUT1 + D // NT * 8
C_DOWN1 = C_UP1 + 2 * FF // NT * 8
C_PROJ = C_DOWN1 + D // NT * FKT // 2
C_PLE = C_PROJ + D // NT
C_IN2 = C_PLE + D // NT * 8
C_BR = C_IN2 + 8704 // NT * 8
C_OUT2 = C_BR + D // NT * 8
C_UP2 = C_OUT2 + D // NT * 8
C_DOWN2 = C_UP2 + 2 * FF // NT * 8
C_END = C_DOWN2 + D // NT * FKT // 2

A_IN1 = 1
A_OUT1 = A_IN1 + 6
A_UP1 = A_OUT1 + 2
A_DOWN1 = A_UP1 + 11
A_PROJ = A_DOWN1 + 2
A_PLE = A_PROJ + 2
A_IN2 = A_PLE + 2
A_BR = (A_IN2 + 9, A_IN2 + 8)
A_OUT2 = (A_BR[0] + 4, A_BR[1] + 4)
A_UP2 = (A_OUT2[0] + 2, A_OUT2[1] + 2)
A_DOWN2 = (A_UP2[0] + 11, A_UP2[1] + 11)

G_X1 = 0
G_Y1 = G_X1 + 8
G_F1 = G_Y1 + 8
G_P = G_F1 + 8
G_PLE = G_P + 1
G_X2 = G_PLE + 8
G_Y2 = G_X2 + 8
G_M2 = G_Y2 + 8
G_F2 = G_M2 + 8

X_PLE, X_NORM = 0, 4

N_IN1, N_F1, N_PLE, N_END1, N_IN2, N_F2, N_END2 = range(7)

GV_NEG = 4
GV_LA = GV_NEG + 2
GV_KE = GV_LA + 1
GV_QK = GV_KE + 8
GV_ST1 = GV_QK + 4
GV_ST2 = GV_ST1 + 8
GV_OSM = GV_ST2 + 3
GV_END = GV_OSM + 9
GA_SILU = 5
GA_ATTN = 6

SCORES_FREE = 3 * P
NEG = -1e30
MASKED = -3e38


def pair(v, p):
    return v[p] if isinstance(v, tuple) else v


def two_blocks_kernel(nc, x, p, norm_mix_w, w_in, rel_bias, w_gate_up, b_gate, gla_norm_w, w_out, norm_ffn_w,
                      w_up, w_conv, b_conv, w_down, norm_ple_w, w_ple_gate, w_ple_proj, final_w,
                      norm_mix_g2, w_in2, sinks, w_bra, w_brb, w_out2, norm_ffn_g2, w_up2, w_down2, final_g2, out):
    ctx = ExitStack()
    with ctx:
        def sem(name):
            return ctx.enter_context(nc.semaphore(name))

        place = [nc.sbuf_base + (-nc.sbuf_base) % 64]

        def sb(name, shape, dt=F32, at=None):
            size = 4
            for n in shape[1:]:
                size *= n
            size += -size % 64
            if at is None:
                at = place[0]
                place[0] += size
            else:
                ends.append(at + size)
            return nc.alloc_sbuf_tensor_at(name, shape, dt, offset=at)

        ends = []
        X = sb("X", [P, TB, D])
        stationary = place[0]
        AH = sb("AH", [P, KT, T], F32R)
        AL = sb("AL", [P, KT, T], F32R)
        WR = sb("WR", [P, RING, CHUNK_KT, NT])
        WH = sb("WH", [P, RING, CHUNK_KT, NT], F32R)
        WL = sb("WL", [P, RING, CHUNK_KT, NT], F32R)
        ident = sb("ident", [P, P])
        tri_le = sb("tri_le", [P, P])
        tri_gt = sb("tri_gt", [P, P])
        neg_tri = sb("neg_tri", [P, P])
        neg_ones = sb("neg_ones", [P, P])
        neg_mask = sb("neg_mask", [P, P])
        vec = sb("vec", [P, 6 * KT + 4 * 2 * FKT])
        nw = vec[:, 0:6 * KT].rearrange("p (n k) -> p n k", k=KT)
        cw = vec[:, 6 * KT:].rearrange("p (n k) -> p n k", k=2 * FKT)
        junk = sb("junk", [P, NT])
        ss = sb("ss", [P, TB, 4])
        ssum = sb("ssum", [P, TB])
        smean = sb("smean", [P, TB])
        sroot = sb("sroot", [P, TB])
        inv = sb("inv", [P, 7, TB])
        base = place[0]
        P1 = sb("P1", [P, TB, GATE1], at=base)
        o1 = base + TB * GATE1 * 4
        BIAS = sb("BIAS", [P, HEADS, 3 * P], at=o1)
        QK = sb("QK", [P, PAIRS, 2, T], at=o1 + 24576)
        o2 = o1 + 24576 + 16384
        SB = sb("SB", [P, 2, SCORES_FREE], at=o2)
        PB = sb("PB", [P, 2, SCORES_FREE], at=o2 + 3072)
        PT = sb("PT", [P, 2, SCORES_FREE], at=o2 + 6144)
        nmax = sb("nmax", [P, HEADS, 2], at=o2 + 9216)
        rsum = sb("rsum", [P, HEADS, 2], at=o2 + 9344)
        rrec = sb("rrec", [P, HEADS, 2], at=o2 + 9472)
        rmax = sb("rmax", [P, HEADS, 2], at=o2 + 9600)
        glT = sb("glT", [RANK, T], at=o1 + 51200)
        wgu = sb("wgu", [RANK, GLA_KW], at=o1 + 52224)
        bgb = sb("bgb", [P, GLA_KW], at=o1 + 55424)
        LG = sb("LG", [P, TB, GLA_KW], at=o2 + 1024)
        LM = sb("LM", [P, TB, GLA_KW], at=o2 + 5120)
        LA = sb("LA", [P, TB, GLA_KW], at=stationary)
        EB = sb("EB", [P, GLA_HEADS, T], at=stationary + 4096)
        EN = sb("EN", [P, GLA_HEADS, T], at=stationary + 8192)
        QD = sb("QD", [P, GLA_HEADS, T], at=o1 + 25600)
        KI = sb("KI", [P, GLA_HEADS, T], at=o1 + 29696)
        KE = sb("KE", [P, TB, GLA_KW], at=o1 + 33792)
        AT = sb("AT", [P, TB * GLA_HEADS, P], at=o1 + 37888)
        ST = sb("ST", [P, 3, GLA_HEADS, GLA_DV], at=o1 + 41984)
        gnw = sb("gnw", [P, GLA_DV], at=o1 + 55424)
        osq = sb("osq", [P, TB, GLA_HEADS], at=o1 + 56448)
        osm = sb("osm", [P, TB, GLA_HEADS], at=o1 + 56512)
        osr = sb("osr", [P, TB, GLA_HEADS], at=o1 + 56576)
        oiv = sb("oiv", [P, TB, GLA_HEADS], at=o1 + 56640)
        SR = sb("SR", [P, TB, GLA_W], at=o1 + 8192)
        WG = sb("WG", [P, KT, RANK], at=o1 + 54400)
        WGH = sb("WGH", [P, KT * RANK + P - RANK], F32R, at=o1 + 41984)
        WGL = sb("WGL", [P, KT * RANK + P - RANK], F32R, at=o1 + 43520)
        ZH = sb("ZH", [P, KT, T], F32R, at=o1)
        ZL = sb("ZL", [P, KT, T], F32R, at=o1 + 16384)
        BH = sb("BH", [P, FKT, T], F32R, at=base)
        BL = sb("BL", [P, FKT, T], F32R, at=base + FKT * T * 4)
        o3 = base + 2 * FKT * T * 4
        U = sb("U", [P, 2, TB, NT], at=o3)
        CV = sb("CV", [P, 2, 4, T], at=o3 + 8192)
        SG = sb("SG", [P, TB, NT], at=o3)
        HB = sb("HB", [P, TB, NT], at=o3 + 4096)
        pin = sb("pin", [P, TB, T], at=o3)
        PTH = sb("PTH", [P, CHUNK_KT, T], F32R, at=o3 + 2048)
        PTL = sb("PTL", [P, CHUNK_KT, T], F32R, at=o3 + 4096)
        fw2 = sb("fw2", [P, D], at=o3)
        norm_rows = sb("norm_rows", [6 * KT, P], at=base)
        conv_rows = sb("conv_rows", [2 * FKT, 4, P], at=base + 512)
        PP = sb("PP", [P, TB, D], at=base)
        GT = sb("GT", [P, TB, NT], at=base + 16384)
        fw = sb("fw", [P, D], at=base + 20480)
        PQ = sb("PQ", [P, TB, GATES2], at=base)
        PG = sb("PG", [P, TB, 2 * D], at=base + TB * GATES2 * 4)
        o4 = base + TB * GATES2 * 4 + TB * 2 * D * 4
        QT2 = sb("QT2", [P, PAIRS, T], at=stationary + 4096)
        KD = sb("KD", [P, TB, KV_HEADS, 2, HD], at=stationary)
        KT2 = sb("KT2", [P, KV_HEADS, T], at=stationary + 12288)
        SB2 = sb("SB2", [P, 2, SCORES_FREE], at=o4 + 16384)
        PB2 = sb("PB2", [P, 2, SCORES_FREE], at=o4 + 19456)
        PT2 = sb("PT2", [P, 2, SCORES_FREE], at=o4 + 22528)
        nmax2 = sb("nmax2", [P, HEADS, 2], at=o4 + 25600)
        rsum2 = sb("rsum2", [P, HEADS, 2], at=o4 + 25728)
        rrec2 = sb("rrec2", [P, HEADS, 2], at=o4 + 25856)
        rmax2 = sb("rmax2", [P, HEADS, 2], at=o4 + 25984)
        sk = sb("sk", [P, HEADS], at=o4 + 32768)
        sk2 = sb("sk2", [P, HEADS, 2], at=o4 + 32832)
        dist = sb("dist", [P, 2 * P], at=o4 + 32960)
        QKB = sb("QKB", [P, PAIRS, 2, T], at=stationary + 16384)
        SM = sb("SM", [P, 4, SCORES_FREE], at=o4)
        SE = sb("SE", [P, 4, SCORES_FREE], at=o4 + 6144)
        SA = sb("SA", [P, 2, SCORES_FREE], at=o4 + 12288)
        XH = sb("XH", [P, KT, T], F32R, at=o4)
        XL = sb("XL", [P, KT, T], F32R, at=o4 + 16384)
        MH = sb("MH", [P, KT, T], F32R, at=base)
        ML = sb("ML", [P, KT, T], F32R, at=base + 16384)
        assert max(ends) <= nc.sbuf_usable_end, (max(ends), nc.sbuf_usable_end)

        acc = ctx.enter_context(nc.psum_tensor("acc", [P, 2, TB, NT], F32))
        tp = ctx.enter_context(nc.psum_tensor("tp", [P, 4, NT], F32))

        def acc_bank(n):
            return acc[:, n // 2, n % 2, :]

        w_loaded = [sem(f"w_loaded{s}") for s in range(RING)]
        hi_done, lo_done, chunk_used = sem("hi_done"), sem("lo_done"), sem("chunk_used")
        acc_free = [sem("acc_free0"), sem("acc_free1")]
        turned, turned_hi, turned_lo = sem("turned"), sem("turned_hi"), sem("turned_lo")
        x_in = [sem(f"x_in{n}") for n in range(D // NT)]
        x_scaled, squared, sums, mean, root, inv_ready = (
            sem("x_scaled"), sem("squared"), sem("sums"), sem("mean"), sem("root"), sem("inv_ready"))
        norms_in, convs_in, masks, mask_step = sem("norms_in"), sem("convs_in"), sem("masks"), sem("mask_step")
        bias_in, bias_masked = sem("bias_in"), sem("bias_masked")
        qk_turned, qk_copied, qk_copied_v = sem("qk_turned"), sem("qk_copied"), sem("qk_copied_v")
        s_full, s_read, s_max, s_neg, e_done, pt_full, pt_copied, pv_done = (
            sem("s_full"), sem("s_read"), sem("s_max"), sem("s_neg"), sem("e_done"), sem("pt_full"),
            sem("pt_copied"), sem("pv_done"))
        rec_done, y_ready = sem("rec_done"), sem("y_ready")
        gate_in, gate_pad, gate_hi, gate_lo, gate_pe, gate_v, gate_a = (
            sem("gate_in"), sem("gate_pad"), sem("gate_hi"), sem("gate_lo"), sem("gate_pe"), sem("gate_v"),
            sem("gate_a"))
        gla_pe, gla_v, gla_a, gla_p, gla_in = sem("gla_pe"), sem("gla_v"), sem("gla_a"), sem("gla_p"), sem("gla_in")
        p_in, vec_turned, vec_ready = sem("p_in"), sem("vec_turned"), sem("vec_ready")
        u_turned, c_init, tap1, conv_done, gelu_done, h_ready, h_hi, h_lo = (
            sem("u_turned"), sem("c_init"), sem("tap1"), sem("conv_done"), sem("gelu_done"),
            sem("h_ready"), sem("h_hi"), sem("h_lo"))
        hb_turned, hb_hi, hb_lo, g_mul = sem("hb_turned"), sem("hb_hi"), sem("hb_lo"), sem("g_mul")
        fw_in, sk_in, kd_done, sink_v, sink_a = sem("fw_in"), sem("sk_in"), sem("kd_done"), sem("sink_v"), sem("sink_a")
        z_full, m_done, z_read, ez_done, ln_done, sp_done, arg_full, a_done, stick_pv = (
            sem("z_full"), sem("m_done"), sem("z_read"), sem("ez_done"), sem("ln_done"), sem("sp_done"),
            sem("arg_full"), sem("a_done"), sem("stick_pv"))

        def slices_of(count):
            return lambda n: (acc_free[n % 2], pair(count, n % 2) + n // 2 + 1)

        def slices_scaled(first):
            return lambda n: (x_scaled, first + n + 1)

        m_ready = sem("m_ready")
        weighted, last_gates, scaled_act, scaled_dve = sem("weighted"), sem("last_gates"), sem("scaled_act"), sem("scaled_dve")
        inv_both, gnw_in = sem("inv_both"), sem("gnw_in")
        fg_in, out_done = sem("fg_in"), sem("out_done")

        block = ctx.enter_context(nc.Block())

        def wide(v, shape):
            return v.to_broadcast(shape)

        def rows(w, kt, cols):
            return w[kt * P:(kt + CHUNK_KT) * P, cols].rearrange("(a p) n -> p a n", p=P)

        def by_row(v):
            return v.rearrange("(k p) -> k p", p=P)

        @block.sync
        def _(sp):
            def load(w, kt, cols, base, j, it=None, per=0):
                n = base + j
                first = it is None and n < RING
                at = n if it is None else n + per * it
                if not first:
                    sp.wait_ge(hi_done, at - RING + 1)
                    sp.wait_ge(lo_done, at - RING + 1)
                sp.dma_start(WR[:, n % RING], rows(w, kt, cols)).then_inc(w_loaded[n % RING], 16)

            def tile(w, col, nk, base, j0, it=None, per=0, kt0=0):
                for q in range(nk // CHUNK_KT):
                    load(w, kt0 + CHUNK_KT * q, bass.ds(col, NT), base, j0 + q, it, per)

            def plain(w, base, n0, n1):
                with sp.Fori(n0, n1) as n:
                    tile(w, n * NT, KT, base, 0, n, 8)

            for n, w in enumerate((norm_mix_w, norm_ffn_w, norm_ple_w, norm_mix_g2, norm_ffn_g2, final_w)):
                sp.dma_start(norm_rows[n * KT:(n + 1) * KT, :], by_row(w)).then_inc(norms_in, 16)
            for n in range(D // NT):
                cols = slice(n * NT, (n + 1) * NT)
                sp.dma_start(X[:, :, cols], x[:, cols].rearrange("(a p) n -> p a n", p=P)).then_inc(x_in[n], 16)
                load(w_in, CHUNK_KT * n, slice(0, NT), C_IN1, n)
            for n in range(RING, KT // CHUNK_KT):
                load(w_in, CHUNK_KT * n, slice(0, NT), C_IN1, n)
            plain(w_in, C_IN1, 1, GATE1 // NT)
            plain(w_out, C_OUT1, 0, D // NT)
            with sp.Fori(0, FF // NT) as n:
                tile(w_up, n * NT, KT, C_UP1, 0, n, 16)
                tile(w_up, n * NT + FF, KT, C_UP1, 8, n, 16)
            with sp.Fori(0, D // NT // 2) as n:
                for half in range(2):
                    tile(w_down, n * (2 * NT) + half * NT, FKT, C_DOWN1, half * FKT // 2, n, FKT)
            for n in range(D // NT):
                load(w_ple_proj, 0, bass.ds(n * NT, NT), C_PROJ, n)
            plain(w_ple_gate, C_PLE, 0, D // NT)
            plain(w_in2, C_IN2, 0, 8704 // NT)
            with sp.Fori(0, D // NT) as n:
                tile(w_bra, n * NT, KT // 2, C_BR, 0, n, 8)
                tile(w_brb, n * NT, KT // 2, C_BR, 4, n, 8)
            plain(w_out2, C_OUT2, 0, D // NT)
            with sp.Fori(0, FF // NT) as n:
                tile(w_up2, n * NT, KT, C_UP2, 0, n, 16)
                tile(w_up2, n * NT + FF, KT, C_UP2, 8, n, 16)
            with sp.Fori(0, D // NT // 2) as n:
                for half in range(2):
                    tile(w_down2, n * (2 * NT) + half * NT, FKT, C_DOWN2, half * FKT // 2, n, FKT)
            for n, ready, count in ((0, scaled_act, 1), (3, scaled_dve, 1), (1, scaled_act, 2), (2, scaled_dve, 2)):
                sp.wait_ge(ready, count)
                sp.dma_start(out[:, n * NT:(n + 1) * NT].rearrange("(a p) n -> p a n", p=P),
                             X[:, :, n * NT:(n + 1) * NT]).then_inc(out_done, 16)
            sp.wait_ge(out_done, 16 * (D // NT))

        @block.gpsimd
        def _(pool):
            pool.memset(ident[:], 0.0).then_inc(mask_step, 1)
            pool.wait_ge(mask_step, 1)
            pool.affine_select(out=ident[:], in_=ident[:], compare_op=ALU.not_equal, fill=1.0, base=0,
                               pattern=[[-1, P]], channel_multiplier=1).then_inc(masks, 1)
            for tap in range(3):
                pool.dma_start(conv_rows[:, tap], by_row(w_conv[tap])).then_inc(convs_in, 16)
            pool.dma_start(conv_rows[:, 3], by_row(b_conv)).then_inc(convs_in, 16)
            pool.dma_start(WG[:], w_in[:, GATE1:GATE1 + RANK].rearrange("(k p) n -> p k n", p=P)).then_inc(gate_in, 16)
            pool.dma_start(wgu[:], w_gate_up).then_inc(gla_in, 16)
            pool.dma_start(bgb[:], b_gate.partition_broadcast(P)).then_inc(gla_in, 16)
            pool.memset(tri_le[:], 1.0).then_inc(mask_step, 1)
            pool.memset(tri_gt[:], 1.0).then_inc(mask_step, 1)
            pool.memset(neg_tri[:], -1.0).then_inc(mask_step, 1)
            pool.memset(neg_mask[:], 0.0).then_inc(mask_step, 1)
            pool.memset(neg_ones[:], -1.0).then_inc(masks, 1)
            pool.wait_ge(mask_step, 5)
            pool.affine_select(out=neg_tri[:], in_=neg_tri[:], compare_op=ALU.is_ge, fill=0.0, base=0,
                               pattern=[[-1, P]], channel_multiplier=1).then_inc(masks, 1)
            pool.affine_select(out=neg_mask[:], in_=neg_mask[:], compare_op=ALU.is_ge, fill=NEG, base=-1,
                               pattern=[[1, P]], channel_multiplier=-1).then_inc(masks, 1)
            pool.affine_select(out=tri_le[:], in_=tri_le[:], compare_op=ALU.is_ge, fill=0.0, base=0,
                               pattern=[[1, P]], channel_multiplier=-1).then_inc(mask_step, 1)
            pool.affine_select(out=tri_gt[:], in_=tri_gt[:], compare_op=ALU.is_ge, fill=0.0, base=-1,
                               pattern=[[-1, P]], channel_multiplier=1).then_inc(mask_step, 1)
            pool.wait_ge(mask_step, 7)
            pool.memset(tri_le[0:LOOK, LOOK:P], 0.0).then_inc(masks, 1)
            pool.memset(tri_gt[LOOK:P, 0:LOOK], 0.0).then_inc(masks, 1)
            pool.wait_ge(chunk_used, 8)
            pool.dma_start(BIAS[:], bass.AP(tensor=rel_bias.tensor, offset=1,
                                            ap=[[1, P], [2 * MAX_REL + 1, HEADS], [1, 3 * P]])).then_inc(bias_in, 16)
            pool.wait_ge(bias_in, 16)
            pool.memset(BIAS[0:LOOK, :, P:P + LOOK], MASKED).then_inc(bias_masked, 1)
            pool.wait_ge(y_ready, 4)
            pool.dma_start(gnw[:], gla_norm_w.partition_broadcast(P)).then_inc(gnw_in, 16)
            pool.memset(AT[:], 0.0).then_inc(gla_p, 1)
            pool.wait_ge(gla_a, GA_ATTN)
            pool.affine_select(out=AT[:], in_=AT[:], compare_op=ALU.is_ge, fill=0.0, base=0,
                               pattern=[[0, TB * GLA_HEADS], [1, P]], channel_multiplier=-1).then_inc(gla_p, 1)
            pool.wait_ge(h_lo, FF // NT)
            pool.dma_start(pin[:], p.rearrange("(a p) n -> p a n", p=P)).then_inc(p_in, 16)
            pool.wait_ge(chunk_used, C_PROJ)
            pool.dma_start(fw[:], final_w.partition_broadcast(P)).then_inc(fw_in, 16)
            pool.dma_start(sk[:], sinks.partition_broadcast(P)).then_inc(sk_in, 16)
            pool.iota(dist[:], pattern=[[-1, 2 * P]], base=P, channel_multiplier=1,
                      allow_small_or_imprecise_dtypes=True).then_inc(kd_done, 1)
            pool.wait_ge(kd_done, 1)
            pool.affine_select(out=dist[:], in_=dist[:], compare_op=ALU.is_ge, fill=-NEG, base=P,
                               pattern=[[-1, 2 * P]], channel_multiplier=1).then_inc(kd_done, 1)
            pool.wait_ge(kd_done, 2)
            pool.affine_select(out=dist[:], in_=dist[:], compare_op=ALU.is_ge, fill=-NEG, base=-1,
                               pattern=[[1, 2 * P]], channel_multiplier=-1).then_inc(kd_done, 1)
            pool.wait_ge(acc_free[0], A_IN2 + 2)
            for tb in range(TB):
                for twin in range(2):
                    pool.tensor_copy(KD[:, tb, :, twin, :], PQ[:, tb, KA2:KA2 + KV_HEADS * HD]
                                     .rearrange("p (g d) -> p g d", d=HD)).then_inc(kd_done, 1)

            pool.wait_ge(hb_lo, 2 * (FF // NT))
            pool.dma_start(fw2[:], final_g2.partition_broadcast(P)).then_inc(fg_in, 16)

        @block.tensor
        def _(pe):
            def chunk(H, L, kt, base, j, a, first, last, it=None, per=0):
                n = base + j
                pe.wait_ge(lo_done, (n if it is None else n + per * it) + 1)
                for k in range(CHUNK_KT):
                    for tb in range(TB):
                        cols = slice(tb * P, (tb + 1) * P)
                        o, s = acc[:, a, tb, :], n % RING
                        begin, end = first and k == 0, last and k == CHUNK_KT - 1
                        pe.matmul(o, H[:, kt + k, cols], WH[:, s, k], start=begin, stop=False)
                        pe.matmul(o, H[:, kt + k, cols], WL[:, s, k], start=False, stop=False)
                        mm = pe.matmul(o, L[:, kt + k, cols], WH[:, s, k], start=False, stop=end)
                mm.then_inc(chunk_used, 1)

            def tile(H, L, nk, base, j0, a, count, it=None, per=0, each=1, kt0=0, between=None, groups=None):
                pe.wait_ge(acc_free[a], count if it is None else count + each * it)
                for q in range(nk // CHUNK_KT):
                    if groups is not None:
                        pe.wait_ge(turned_lo, groups + kt0 // 2 + q + 1)
                    chunk(H, L, kt0 + CHUNK_KT * q, base, j0 + q, a, q == 0, q == nk // CHUNK_KT - 1, it, per)
                    if between is not None:
                        between(q)

            def turn(src, group, gs, ready=None):
                for g in gs:
                    n = group + g
                    if ready is not None and g % 2 == 0:
                        pe.wait_ge(*ready(g // 2))
                    if n >= 4:
                        pe.wait_ge(turned_lo, n - 3)
                    for k in range(2):
                        for tb in range(TB):
                            mm = pe.transpose(tp[:, n % 4, k * T + tb * P:k * T + (tb + 1) * P],
                                              src(2 * g + k, tb), ident[:])
                    mm.then_inc(turned, 1)

            def x_cols(kt, tb):
                return X[:, tb, kt * P:(kt + 1) * P]

            def turn_ahead(src, group, ready, q0):
                def go(q):
                    if q0 <= q < q0 + 4:
                        turn(src, group, [q - q0], ready)
                return go

            def turned_tile(src, group, H, L, nk, base, a, count, ready=None, ahead=False, also=None):
                if not ahead:
                    turn(src, group, range(4), ready)

                def rest(q):
                    if also is not None:
                        also(q)
                    if q < 4 and nk == KT:
                        turn(src, group, [4 + q], ready)
                    elif q < 2:
                        turn(src, group, [4 + 2 * q, 5 + 2 * q], ready)

                tile(H, L, nk, base, 0, a, count, groups=group, between=rest)

            def loop_tiles(H, L, base, count, i0, i1, nk):
                with pe.Fori(i0, i1) as i:
                    tile(H, L, nk, base, 0, 0, pair(count, 0), i, nk)
                    tile(H, L, nk, base, nk // 2, 1, pair(count, 1), i, nk)

            def four_tiles(src, group, H, L, base, count, ready=None, ahead=False, after=None):
                turned_tile(src, group, H, L, KT, base, 0, pair(count, 0), ready, ahead)
                for n in range(1, D // NT):
                    tile(H, L, KT, base, 8 * n, n % 2, pair(count, n % 2) + n // 2,
                         between=after if n == D // NT - 1 else None)

            def scores(h, n, q_of, k_of):
                if n >= 2:
                    pe.wait_ge(s_read, n - 1)
                o = tp[:, n % 2, :]
                pe.matmul(o[:, 0:P], q_of(h, 0, P), k_of(h, 0, P), start=True, stop=True)
                pe.matmul(o[:, P:3 * P], q_of(h, P, T), k_of(h, 0, T), start=True, stop=True).then_inc(s_full, 1)

            def turn_weights(n, B):
                pe.wait_ge(e_done, n + 1)
                if n >= 2:
                    pe.wait_ge(pt_copied, n - 1)
                for b in range(3):
                    mm = pe.transpose(tp[:, 2 + n % 2, b * P:(b + 1) * P], B[:, n % 2, b * P:(b + 1) * P], ident[:])
                mm.then_inc(pt_full, 1)

            def weigh(h, n, B, v_of):
                pe.wait_ge(pt_copied, n + 1)
                for qb in range(TB):
                    o = acc_bank(2 * qb + h // 8)[:, (h % 8) * HD:(h % 8 + 1) * HD]
                    for kb in range(qb + 1):
                        blk = qb + kb
                        mm = pe.matmul(o, B[:, n % 2, blk * P:(blk + 1) * P], v_of(h, kb),
                                       start=(kb == 0), stop=(kb == qb))
                mm.then_inc(pv_done, 1)

            def softmax_attention(n0, q_of, k_of, v_of, EXP, TURNED):
                for h in range(HEADS):
                    turn_weights(n0 + h, EXP)
                    if h + 2 < HEADS:
                        scores(h + 2, n0 + h + 2, q_of, k_of)
                    weigh(h, n0 + h, TURNED, v_of)

            pe.wait_ge(masks, 1)
            pe.wait_ge(norms_in, 16 * 6)
            pe.transpose(acc_bank(3)[:, 0:6 * KT], norm_rows[:],
                         ident[0:6 * KT, 0:6 * KT]).then_inc(vec_turned, 1)

            def turn_convs(q):
                if q != 6:
                    return
                pe.wait_ge(convs_in, 16 * 4)
                for n in range(4):
                    mm = pe.transpose(acc_bank(2)[:, n * 2 * FKT:(n + 1) * 2 * FKT], conv_rows[:, n, :],
                                      ident[0:2 * FKT, 0:2 * FKT])
                mm.then_inc(vec_turned, 1)

            turned_tile(x_cols, G_X1, AH, AL, KT, C_IN1, 0, A_IN1, lambda n: (x_in[n], 16), also=turn_convs)
            pe.wait_ge(masks, 6)
            tile(AH, AL, KT, C_IN1, 8, 1, A_IN1)
            loop_tiles(AH, AL, C_IN1, A_IN1, 1, GATE1 // NT // 2 - 1, KT)

            def turn_four(m, block_of):
                if m >= 4:
                    pe.wait_ge((qk_copied, qk_copied_v)[m % 2], (m - 4) // 2 + 1)
                for b in range(4):
                    mm = pe.transpose(tp[:, m % 4, b * P:(b + 1) * P], block_of(b // TB, b % TB), ident[:])
                mm.then_inc(qk_turned, 1)

            def turn_band(q):
                turn_four(q, lambda b, tb: P1[:, tb, (QA1, KA1)[b] + q * P:(QA1, KA1)[b] + (q + 1) * P])

            def half(h):
                return slice((h % 2) * HD, (h % 2 + 1) * HD)

            def q_band(h, a, b):
                return QK[half(h), h // 2, 0, a:b]

            def k_band(h, a, b):
                return QK[half(h), h // 2, 1, a:b]

            def gate_logits(q):
                if q == 0:
                    pe.wait_ge(qk_copied, 4)
                    pe.wait_ge(qk_copied_v, 4)
                    pe.wait_ge(gate_lo, 1)
                    for k in range(KT):
                        cols = slice(k * RANK, k * RANK + P)
                        pe.matmul(tp[:, 0, 0:T], WGH[:, cols], AH[:, k], start=(k == 0), stop=False)
                        pe.matmul(tp[:, 0, 0:T], WGH[:, cols], AL[:, k], start=False, stop=False)
                        mm = pe.matmul(tp[:, 0, 0:T], WGL[:, cols], AH[:, k], start=False, stop=(k == KT - 1))
                    mm.then_inc(gate_pe, 1)
                if q == 3:
                    pe.wait_ge(gate_v, 1)
                    pe.wait_ge(gla_in, 32)
                    for tb in range(TB):
                        mm = pe.matmul(tp[:, 2 + tb, :], glT[:, tb * P:(tb + 1) * P], wgu[:], start=True, stop=True)
                    mm.then_inc(gla_pe, 1)
                if q == 6:
                    scores(0, 0, q_band, k_band)
                    scores(1, 1, q_band, k_band)

            n = GATE1 // NT // 2 - 1
            tile(AH, AL, KT, C_IN1 + 16 * n, 0, 0, A_IN1 + n, between=turn_band)
            tile(AH, AL, KT, C_IN1 + 16 * n, 8, 1, A_IN1 + n, between=gate_logits)
            pe.wait_ge(acc_free[0], A_OUT1)
            pe.wait_ge(acc_free[1], A_OUT1)

            pe.wait_ge(gla_v, GV_NEG)
            softmax_attention(0, q_band, k_band, lambda h, kb: P1[:, kb, VA1 + h * HD:VA1 + (h + 1) * HD], PB, PT)
            def y1_cols(kt, tb):
                col = kt * P if kt < KT // 2 else RG1 + (kt - KT // 2) * P
                return P1[:, tb, col:col + P]

            for h in range(GLA_HEADS):
                for m, col in enumerate((QG1, KG1)):
                    for tb in range(TB):
                        mm = pe.transpose(tp[:, h, m * T + tb * P:m * T + (tb + 1) * P],
                                          P1[:, tb, col + h * P:col + (h + 1) * P], ident[:])
            mm.then_inc(gla_pe, 1)
            pe.wait_ge(y_ready, 4)
            for tb in range(TB):
                mm = pe.matmul(acc_bank(tb), tri_gt[:], LA[:, tb, :], start=True, stop=True)
            mm.then_inc(gla_pe, 1)
            for tb in range(TB):
                for h in range(GLA_HEADS):
                    mm = pe.matmul(acc_bank(2 + h // 2)[:, (h % 2) * T + tb * P:(h % 2) * T + (tb + 1) * P],
                                   LA[:, tb, h * P:(h + 1) * P], tri_le[:], start=True, stop=True)
            mm.then_inc(gla_pe, 1)
            pe.wait_ge(gla_v, GV_KE)
            for c in range(3):
                rows_c = slice((c % 2) * LOOK, (c % 2 + 1) * LOOK)
                if c == 1:
                    pe.wait_ge(gla_a, 4)
                if c == 2:
                    pe.wait_ge(gla_v, GV_ST1)
                for h in range(GLA_HEADS):
                    mm = pe.matmul(acc_bank(2 * (c % 2) + h // 2)[:, (h % 2) * GLA_DV:(h % 2 + 1) * GLA_DV],
                                   KE[rows_c, c // 2, h * P:(h + 1) * P],
                                   P1[rows_c, c // 2, VG1 + h * GLA_DV:VG1 + (h + 1) * GLA_DV], start=True, stop=True)
                mm.then_inc(gla_pe, 1)
            for tb in range(TB):
                for h in range(GLA_HEADS):
                    cols = slice(tb * P, (tb + 1) * P)
                    mm = pe.matmul(tp[:, tb, h * P:(h + 1) * P], KI[:, h, cols], QD[:, h, cols], start=True, stop=True)
            mm.then_inc(gla_pe, 1)
            pe.wait_ge(gla_a, GA_ATTN)
            turn(y1_cols, G_Y1, range(4))
            pe.wait_ge(gla_p, 2)
            pe.wait_ge(gla_v, GV_ST2)
            for tb in range(TB):
                for h in range(GLA_HEADS):
                    o = acc_bank(2 * tb + h // 2)[:, (h % 2) * GLA_DV:(h % 2 + 1) * GLA_DV]
                    first = pe.matmul(o, AT[:, tb * GLA_HEADS + h, :],
                                      P1[:, tb, VG1 + h * GLA_DV:VG1 + (h + 1) * GLA_DV],
                                      start=(h % 2 == 0), stop=True, skip_group_check=True)
                    for half_ in range(2):
                        c = 2 * tb + half_
                        if c == 0:
                            continue
                        mm = pe.matmul(o[half_ * LOOK:(half_ + 1) * LOOK, :],
                                       QD[:, h, c * LOOK:(c + 1) * LOOK], ST[:, c - 1, h, :],
                                       start=False, stop=True, skip_group_check=True)
                mm.then_inc(gla_pe, 1)
            pe.wait_ge(gla_v, GV_END - GLA_HEADS)
            four_tiles(y1_cols, G_Y1, ZH, ZL, C_OUT1, A_OUT1, lambda n: (gla_v, GV_END), ahead=True,
                       after=turn_ahead(x_cols, G_F1, slices_of(A_OUT1), 2))

            def turn_u(a, it, first):
                def go(q):
                    if q != 1:
                        return
                    pe.wait_ge(acc_free[a], A_UP1 + it + 1)
                    if not first:
                        pe.wait_ge(h_lo, it)
                    for fb in range(4):
                        for tb in range(TB):
                            mm = pe.transpose(tp[:, 2 * a + fb // 2, (fb % 2) * T + tb * P:(fb % 2) * T + (tb + 1) * P],
                                              U[:, a, tb, fb * P:(fb + 1) * P], ident[:])
                        if fb % 2:
                            mm.then_inc(u_turned, 1)
                return go

            turned_tile(x_cols, G_F1, AH, AL, KT, C_UP1, 0, A_UP1, slices_of(A_OUT1), ahead=True)
            tile(AH, AL, KT, C_UP1, 8, 1, A_UP1, between=turn_u(0, 0, True))
            tile(AH, AL, KT, C_UP1, 16, 0, A_UP1 + 1, between=turn_u(1, 0, True))
            tile(AH, AL, KT, C_UP1, 24, 1, A_UP1 + 1, between=turn_u(0, 1, False))
            with pe.Fori(2, FF // NT) as i:
                tile(AH, AL, KT, C_UP1, 0, 0, A_UP1, i, 16, between=turn_u(1, i - 1, False))
                tile(AH, AL, KT, C_UP1, 8, 1, A_UP1, i, 16, between=turn_u(0, i, False))

            def last_u(q):
                turn_u(1, FF // NT - 1, False)(q)
                if q == (FKT - 4) // CHUNK_KT - 1:
                    pe.wait_ge(h_lo, FF // NT)

            pe.wait_ge(h_lo, FF // NT - 1)

            def turn_p(q):
                if q == 10:
                    pe.wait_ge(p_in, 16)
                    turn(lambda k, tb: pin[:, tb, k * P:(k + 1) * P], G_P, [0])
                turn_ahead(x_cols, G_PLE, slices_of(A_DOWN1), 12)(q)

            for n in range(D // NT):
                tile(BH, BL, FKT, C_DOWN1, n * FKT // 2, n % 2, A_DOWN1 + n // 2,
                     between={0: last_u, D // NT - 1: turn_p}.get(n))
            for n in range(D // NT):
                tile(PTH, PTL, CHUNK_KT, C_PROJ, n, n % 2, A_PROJ + n // 2, groups=G_P)
            four_tiles(x_cols, G_PLE, AH, AL, C_PLE, A_PLE, slices_of(A_DOWN1), ahead=True,
                       after=turn_ahead(x_cols, G_X2, slices_scaled(X_PLE), 3))
            turned_tile(x_cols, G_X2, XH, XL, KT, C_IN2, 0, A_IN2, slices_scaled(X_PLE), ahead=True)
            tile(XH, XL, KT, C_IN2, 8, 1, A_IN2)
            loop_tiles(XH, XL, C_IN2, A_IN2, 1, 7, KT)

            def turn_stick(q):
                turn_four(PAIRS + q, lambda b, tb: PQ[:, tb, (QB2, KB2)[b] + q * P:(QB2, KB2)[b] + (q + 1) * P])

            def q_window(h, a, b):
                return QT2[half(h), h // 2, a:b]

            def k_window(h, a, b):
                return KT2[half(h), h // GROUP, a:b]

            def turn_window(q):
                if q < 4:
                    turn_four(2 * PAIRS + q, lambda b, tb: PQ[:, tb, QA2 + (2 * q + b) * P:QA2 + (2 * q + b + 1) * P])
                elif q < 6:
                    pe.wait_ge(kd_done, 7)
                    turn_four(2 * PAIRS + q,
                              lambda b, tb: KD[:, tb, 2 * (q - 4) + b, :, :].rearrange("p a b -> p (a b)"))
                elif q == 6:
                    pe.wait_ge(qk_copied, 11)
                    pe.wait_ge(qk_copied_v, 11)
                    scores(0, HEADS, q_window, k_window)
                    scores(1, HEADS + 1, q_window, k_window)

            tile(XH, XL, KT, C_IN2, 112, 0, A_IN2 + 7)
            tile(XH, XL, KT, C_IN2, 120, 1, A_IN2 + 7, between=turn_stick)
            tile(XH, XL, KT, C_IN2, 128, 0, A_IN2 + 8, between=turn_window)
            pe.wait_ge(acc_free[0], A_BR[0])
            pe.wait_ge(acc_free[1], A_BR[1])
            softmax_attention(HEADS, q_window, k_window,
                              lambda h, kb: PQ[:, kb, VA2 + (h // GROUP) * HD:VA2 + (h // GROUP + 1) * HD], PB2, PT2)
            def logits(q):
                for h in (2 * q, 2 * q + 1):
                    if h >= 4:
                        pe.wait_ge(a_done, h - 3)
                    z = tp[:, h % 4, :]
                    pe.matmul(z[:, 0:T], QKB[half(h), h // 2, 1, 0:P], QKB[half(h), h // 2, 0, 0:T],
                              start=True, stop=False, skip_group_check=True)
                    pe.matmul(z[:, T:3 * P], QKB[half(h), h // 2, 1, P:T], QKB[half(h), h // 2, 0, P:T],
                              start=False, stop=False, skip_group_check=True)
                    pe.matmul(z[:, 0:P], ident[:], neg_mask[:], start=False, stop=False, skip_group_check=True)
                    pe.matmul(z[:, T:3 * P], ident[:], neg_mask[:], start=False, stop=True,
                              skip_group_check=True).then_inc(z_full, 1)

            pe.wait_ge(s_read, 2 * HEADS)
            logits(0)
            pe.wait_ge(pt_copied, 2 * HEADS)
            logits(1)
            pe.wait_ge(y_ready, 8)
            for q in range(PAIRS):
                for h in (2 * q, 2 * q + 1):
                    pe.wait_ge(sp_done, h + 1)
                    z, i = tp[:, h % 4, :], h % 4
                    pe.matmul(z[:, 0:T], neg_tri[:], SE[:, i, 0:T], start=False, stop=False, skip_group_check=True)
                    pe.matmul(z[:, T:3 * P], neg_tri[:], SE[:, i, T:3 * P], start=False, stop=False,
                              skip_group_check=True)
                    pe.matmul(z[:, P:T], neg_ones[:], SE[:, i, T:3 * P], start=False, stop=True,
                              skip_group_check=True).then_inc(arg_full, 1)
                if q + 2 < PAIRS:
                    logits(q + 2)
                for h in (2 * q, 2 * q + 1):
                    pe.wait_ge(a_done, h + 1)
                    for qb in range(TB):
                        o = acc_bank(2 * qb + h // 8)[:, (h % 8) * HD:(h % 8 + 1) * HD]
                        for kb in range(qb + 1):
                            blk = qb + kb
                            mm = pe.matmul(o, SA[:, h % 2, blk * P:(blk + 1) * P],
                                           PQ[:, kb, VB2 + h * HD:VB2 + (h + 1) * HD], start=(kb == 0), stop=(kb == qb))
                    mm.then_inc(stick_pv, 1)
            pe.wait_ge(y_ready, 12)

            def y2_cols(kt, tb):
                col = QA2 + kt * P if kt < KT // 2 else QB2 + (kt - KT // 2) * P
                return PQ[:, tb, col:col + P]

            turned_tile(y2_cols, G_Y2, AH, AL, KT // 2, C_BR, 0, A_BR[0])
            tile(AH, AL, KT // 2, C_BR, 4, 1, A_BR[1], kt0=KT // 2, groups=G_Y2)
            with pe.Fori(1, D // NT - 1) as i:
                tile(AH, AL, KT // 2, C_BR, 0, 0, A_BR[0], i, 8)
                tile(AH, AL, KT // 2, C_BR, 4, 1, A_BR[1], i, 8, kt0=KT // 2)

            def m_cols(kt, tb):
                return PG[:, tb, kt * P:(kt + 1) * P]

            def slices_merged(n):
                return m_ready, n + 1

            n = D // NT - 1
            tile(AH, AL, KT // 2, C_BR + 8 * n, 0, 0, A_BR[0] + n)
            tile(AH, AL, KT // 2, C_BR + 8 * n, 4, 1, A_BR[1] + n, kt0=KT // 2,
                 between=turn_ahead(m_cols, G_M2, slices_merged, 0))
            four_tiles(m_cols, G_M2, MH, ML, C_OUT2, A_OUT2, slices_merged, ahead=True,
                       after=turn_ahead(x_cols, G_F2, slices_of(A_OUT2), 2))

            def turn_h(it, first):
                def go(q):
                    if q != 1:
                        return
                    pe.wait_ge(acc_free[1], A_UP2[1] + it + 1)
                    if not first:
                        pe.wait_ge(hb_lo, 2 * it)
                    for fb in range(4):
                        for tb in range(TB):
                            mm = pe.transpose(tp[:, fb // 2, (fb % 2) * T + tb * P:(fb % 2) * T + (tb + 1) * P],
                                              HB[:, tb, fb * P:(fb + 1) * P], ident[:])
                        if fb % 2:
                            mm.then_inc(hb_turned, 1)
                return go

            turned_tile(x_cols, G_F2, AH, AL, KT, C_UP2, 0, A_UP2[0], slices_of(A_OUT2), ahead=True)
            tile(AH, AL, KT, C_UP2, 8, 1, A_UP2[1])
            tile(AH, AL, KT, C_UP2, 16, 0, A_UP2[0] + 1, between=turn_h(0, True))
            tile(AH, AL, KT, C_UP2, 24, 1, A_UP2[1] + 1)
            with pe.Fori(2, FF // NT) as i:
                tile(AH, AL, KT, C_UP2, 0, 0, A_UP2[0], i, 16, between=turn_h(i - 1, False))
                tile(AH, AL, KT, C_UP2, 8, 1, A_UP2[1], i, 16)

            def last_h(q):
                turn_h(FF // NT - 1, False)(q)
                if q == (FKT - 4) // CHUNK_KT - 1:
                    pe.wait_ge(hb_lo, 2 * (FF // NT))

            pe.wait_ge(hb_lo, 2 * (FF // NT) - 2)
            tile(BH, BL, FKT, C_DOWN2, 0, 0, A_DOWN2[0], between=last_h)
            tile(BH, BL, FKT, C_DOWN2, FKT // 2, 1, A_DOWN2[1])
            loop_tiles(BH, BL, C_DOWN2, A_DOWN2, 1, 2, FKT)

        @block.scalar
        def _(act):
            def hi(base, js, it=None, per=0):
                for j in js:
                    n = base + j
                    if n >= C_END:
                        continue
                    at = n if it is None else n + per * it
                    act.wait_ge(w_loaded[n % RING], 16 * (n // RING + 1) if it is None
                                else 16 * (n // RING + 1) + 16 * (per // RING) * it)
                    if it is not None or n >= RING:
                        act.wait_ge(chunk_used, at - RING + 1)
                    act.activation(WH[:, n % RING], WR[:, n % RING], ACT.Copy).then_inc(hi_done, 1)

            def turn(H, group, gs, w=None):
                for g in gs:
                    n = group + g
                    act.wait_ge(turned, n + 1)
                    if w is None:
                        last = act.activation(H[:, 2 * g:2 * g + 2, :].rearrange("p a t -> p (a t)"), tp[:, n % 4, :],
                                              ACT.Copy)
                    else:
                        for k in range(2):
                            last = act.activation(H[:, 2 * g + k, :], tp[:, n % 4, k * T:(k + 1) * T], ACT.Copy,
                                                  scale=nw[:, w, 2 * g + k:2 * g + k + 1])
                    last.then_inc(turned_hi, 1)

            def squares(ready, norm, slices=range(4)):
                for n in slices:
                    act.wait_ge(*ready(n))
                    if norm and n == 0:
                        act.wait_ge(sums, norm)
                    for tb in range(TB):
                        k = 8 * norm + 2 * n + tb
                        if k:
                            act.wait_ge(squared, k)
                        act.activation(junk[:], X[:, tb, n * NT:(n + 1) * NT], ACT.Square,
                                       accum_out=ss[:, tb, n:n + 1]).then_inc(squared, 1)

            def sqrt_of(norm):
                act.wait_ge(mean, norm + 1)
                act.activation(sroot[:], smean[:], ACT.Sqrt).then_inc(root, 1)

            def hi_and_turn(base, j0, H, group, gs, w=None):
                for g in gs:
                    hi(base, [j0 + g - gs[0]])
                    turn(H, group, [g], w)

            def start(base, H, group, w, ready, norm, done=0):
                for n in range(4):
                    hi_and_turn(base, 4 + n, H, group, [4 + n], w)
                    if n >= done:
                        squares(ready, norm, [n])
                if done:
                    hi(base, [8])
                sqrt_of(norm)

            def plain(base, n_it, per=16):
                with act.Fori(0, n_it) as i:
                    hi(base, range(4, 4 + per), i, per)

            act.wait_ge(vec_ready, 1)
            for n in range(4):
                turn(AH, G_X1, [n], 0)
                hi(C_IN1, [n])
            start(C_IN1, AH, G_X1, 0, lambda n: (x_in[n], 16), N_IN1)
            act.wait_ge(gate_in, 16)
            act.wait_ge(gate_pad, 1)
            act.activation(WGH[:, 0:KT * RANK], WG[:].rearrange("p k n -> p (k n)"), ACT.Copy).then_inc(gate_hi, 1)
            hi(C_IN1, range(8, 12))
            plain(C_IN1 + 8, 4)

            def copy_pair(M, m, hp):
                if m % 2 == 0:
                    act.wait_ge(qk_turned, m + 1)
                    act.activation(M[:, hp, 0, :], tp[:, m % 4, 0:T], ACT.Copy, scale=HD ** -0.5)
                    act.activation(M[:, hp, 1, :], tp[:, m % 4, T:2 * T], ACT.Copy).then_inc(qk_copied, 1)

            hi(C_IN1, range(76, 84))
            for q in range(PAIRS):
                hi(C_IN1, [84 + q])
                copy_pair(QK, q, q)
            hi(C_IN1, range(92, 96))
            act.wait_ge(gla_v, GV_NEG)
            act.activation(LG[:], LG[:], ACT.Exp).then_inc(gla_a, 1)
            act.wait_ge(gla_a, 1)
            act.activation(LG[:], LG[:], ACT.Ln, bias=1.0).then_inc(gla_a, 1)
            hi(C_IN1, range(96, 99))
            def exps(n, h, S, B, M, R):
                act.wait_ge(s_neg, n + 1)
                if n >= 2:
                    act.wait_ge(pt_full, n - 1)
                act.activation(B[:, n % 2, 0:P], S[:, n % 2, 0:P], ACT.Exp, bias=M[:, h, 0:1],
                               accum_out=R[:, h, 0:1])
                act.activation(B[:, n % 2, P:3 * P], S[:, n % 2, P:3 * P], ACT.Exp, bias=M[:, h, 1:2],
                               accum_out=R[:, h, 1:2]).then_inc(e_done, 1)

            def copy_weights(n, B):
                act.wait_ge(pt_full, n + 1)
                if n >= 2:
                    act.wait_ge(pv_done, n - 1)
                act.activation(B[:, n % 2, :], tp[:, 2 + n % 2, 0:3 * P], ACT.Copy).then_inc(pt_copied, 1)

            exps(0, 0, SB, PB, nmax, rsum)
            hi(C_IN1, [99])
            act.wait_ge(gla_v, GV_LA)
            for h in range(HEADS):
                if h + 1 < HEADS:
                    exps(h + 1, h + 1, SB, PB, nmax, rsum)
                copy_weights(h, PT)
            act.wait_ge(gla_pe, 3)
            for tb in range(TB):
                last = act.activation(KE[:, tb, :], acc_bank(tb), ACT.Exp)
            last.then_inc(gla_a, 1)
            act.wait_ge(gla_pe, 4)
            for h in range(0, GLA_HEADS, 2):
                b = acc_bank(2 + h // 2)
                act.activation(EB[:, h:h + 2, :].rearrange("p a t -> p (a t)"), b, ACT.Exp)
                last = act.activation(EN[:, h:h + 2, :].rearrange("p a t -> p (a t)"), b, ACT.Exp, scale=-1.0)
            last.then_inc(gla_a, 1)
            act.activation(SR[:], P1[:, :, RG1:RG1 + GLA_W], ACT.Silu).then_inc(gla_a, 1)
            act.wait_ge(gla_pe, 8)
            act.wait_ge(gla_p, 1)
            for half_ in range(2):
                part = slice(half_ * LOOK, (half_ + 1) * LOOK)
                for tb in range(TB):
                    last = act.activation(AT[part, tb * GLA_HEADS:(tb + 1) * GLA_HEADS, part],
                                          tp[part, tb, :].rearrange("p (h t) -> p h t", h=GLA_HEADS)[:, :, part],
                                          ACT.Copy)
            last.then_inc(gla_a, 1)
            turn(ZH, G_Y1, range(4))
            act.wait_ge(squared, 8)
            n = 0
            for tb in range(TB):
                act.wait_ge(gla_pe, 9 + tb)
                for h in range(GLA_HEADS):
                    act.wait_ge(gla_a, 6 + n)
                    act.activation(junk[:, 0:GLA_DV], acc_bank(2 * tb + h // 2)[:, (h % 2) * GLA_DV:(h % 2 + 1) * GLA_DV],
                                   ACT.Square, accum_out=osq[:, tb, h:h + 1]).then_inc(gla_a, 1)
                    n += 1
            act.wait_ge(gla_v, GV_OSM)
            act.activation(osr[:], osm[:], ACT.Sqrt).then_inc(gla_a, 1)
            hi_and_turn(C_OUT1, 4, ZH, G_Y1, range(4, 8))
            hi(C_OUT1, range(8, 30))
            hi_and_turn(C_OUT1, 30, AH, G_F1, range(4), 1)
            hi(C_OUT1, range(34, 36))
            start(C_UP1, AH, G_F1, 1, slices_of(A_OUT1), N_F1)
            def evac_u(a, it):
                act.wait_ge(inv_ready, N_F1 + 1)
                act.wait_ge(chunk_used, C_UP1 + 8 * (a + 1) + 16 * it)
                act.activation(U[:, a, 0, :], acc[:, a, 0, :], ACT.Copy, scale=inv[:, N_F1, 0:1])
                act.activation(U[:, a, 1, :], acc[:, a, 1, :], ACT.Copy, scale=inv[:, N_F1, 1:2]).then_inc(acc_free[a], 1)

            def start_conv(a, b, it):
                act.wait_ge(u_turned, 4 * it + 2 * a + b + 1)
                for k in range(2):
                    fb = 2 * b + k
                    f = it * 4 + (a * FKT + fb)
                    last = act.activation(CV[:, a, fb, :], tp[:, 2 * a + b, k * T:(k + 1) * T], ACT.Identity,
                                          bias=cw[:, 3, bass.ds(f, 1)], scale=cw[:, 2, bass.ds(f, 1)])
                last.then_inc(c_init, 1)

            def up1(it, split):
                split(range(8, 12))
                evac_u(0, it)
                split(range(12, 14))
                start_conv(0, 0, it)
                split(range(14, 15))
                start_conv(0, 1, it)
                split(range(15, 17))
                act.wait_ge(conv_done, 4 * it + 2)
                act.activation(CV[:, 0], CV[:, 0], ACT.Gelu_apprx_tanh).then_inc(gelu_done, 1)
                split(range(17, 20))
                evac_u(1, it)
                split(range(20, 22))
                start_conv(1, 0, it)
                split(range(22, 23))
                start_conv(1, 1, it)
                split(range(23, 24))
                act.wait_ge(h_ready, it + 1)
                act.activation(BH[:, bass.ds(it * 4, 4), :], CV[:, 0], ACT.Copy).then_inc(h_hi, 1)

            with act.Fori(0, FF // NT) as i:
                up1(i, lambda js: hi(C_UP1, js, i, 16))
            plain(C_DOWN1 + 4, 18, 4)
            hi(C_DOWN1, [80])
            turn(PTH, G_P, [0])
            hi(C_DOWN1, [81])
            hi_and_turn(C_DOWN1, 82, AH, G_PLE, range(4), 2)
            hi(C_DOWN1, range(86, 92))
            hi(C_PROJ, range(4, 8))
            start(C_PLE, AH, G_PLE, 2, slices_of(A_DOWN1), N_PLE)

            def gate(a, it, first=False):
                act.wait_ge(inv_ready, N_PLE + 1)
                act.wait_ge(chunk_used, C_PLE + 8 * (a + 1) + 16 * it)
                if not first:
                    act.wait_ge(x_scaled, X_PLE + 2 * it + a)
                for tb in range(TB):
                    last = act.activation(GT[:, tb, :], acc[:, a, tb, :], ACT.Sigmoid, scale=inv[:, N_PLE, tb:tb + 1])
                last.then_inc(acc_free[a], 1)

            for n in range(D // NT - 1):
                hi(C_PLE + 8 * n, range(8 if n == 0 else 4, 12))
                gate(n % 2, n // 2, first=(n == 0))
            for n in range(3):
                hi(C_PLE, [28 + n])
                if n < 2:
                    squares(slices_scaled(X_PLE), N_END1, [n])
            hi_and_turn(C_PLE, 31, XH, G_X2, range(4), 3)
            gate(1, 1)
            hi(C_PLE, [35])
            start(C_IN2, XH, G_X2, 3, slices_scaled(X_PLE), N_END1, done=2)
            for n in range(4):
                hi(C_IN2, [9 + n])
                squares(slices_scaled(X_NORM), N_IN2, [n])
            hi(C_IN2, [13])
            sqrt_of(N_IN2)
            hi(C_IN2, range(14, 20))
            plain(C_IN2 + 16, 3)
            act.wait_ge(inv_both, 1)

            def gates(n, a, it):
                act.wait_ge(chunk_used, C_IN2 + 8 * (a + 1) + 16 * it)
                for tb in range(TB):
                    last = act.activation(PG[:, tb, bass.ds(n * NT, NT)], acc[:, a, tb, :], ACT.Sigmoid,
                                          scale=inv[:, N_IN2, tb:tb + 1])
                last.then_inc(acc_free[a], 1)

            hi(C_IN2, range(68, 84))
            gates(0, 1, 4)
            with act.Fori(5, 7) as i:
                hi(C_IN2, range(4, 12), i, 16)
                gates(2 * i - 9, 0, i)
                hi(C_IN2, range(12, 20), i, 16)
                gates(2 * i - 8, 1, i)
            hi(C_IN2, range(116, 124))
            gates(5, 0, 7)
            for q in range(PAIRS):
                hi(C_IN2, [124 + q])
                copy_pair(QKB, PAIRS + q, q)
            gates(6, 1, 7)
            for q in range(PAIRS - 1):
                hi(C_IN2, [132 + q])
                m = 2 * PAIRS + q
                if q in (0, 2):
                    act.wait_ge(qk_turned, m + 1)
                    act.activation(QT2[:, 2 * q:2 * q + 2, :].rearrange("p a t -> p (a t)"), tp[:, m % 4, :], ACT.Copy,
                                   scale=HD ** -0.5).then_inc(qk_copied, 1)
                elif q == 4:
                    act.wait_ge(qk_turned, m + 1)
                    act.activation(KT2[:, 0:2, :].rearrange("p a t -> p (a t)"), tp[:, m % 4, :],
                                   ACT.Copy).then_inc(qk_copied, 1)
            exps(HEADS, 0, SB2, PB2, nmax2, rsum2)
            hi(C_IN2, [139])
            for h in range(HEADS):
                if h + 1 < HEADS:
                    exps(HEADS + h + 1, h + 1, SB2, PB2, nmax2, rsum2)
                copy_weights(HEADS + h, PT2)
            act.wait_ge(sink_v, 1)
            act.activation(sk2[:], sk2[:], ACT.Exp).then_inc(sink_a, 1)
            def exp_z(q):
                for h in (2 * q, 2 * q + 1):
                    act.wait_ge(z_read, h + 1)
                    act.activation(SE[:, h % 4, :], SE[:, h % 4, :], ACT.Exp).then_inc(ez_done, 1)

            def ln_z(q):
                for h in (2 * q, 2 * q + 1):
                    act.wait_ge(ez_done, h + 1)
                    act.activation(SE[:, h % 4, :], SE[:, h % 4, :], ACT.Ln, bias=1.0).then_inc(ln_done, 1)

            exp_z(0)
            ln_z(0)
            for q in range(PAIRS):
                if q + 1 < PAIRS:
                    exp_z(q + 1)
                for h in (2 * q, 2 * q + 1):
                    act.wait_ge(arg_full, h + 1)
                    if h >= 2:
                        act.wait_ge(stick_pv, h - 1)
                    act.activation(SA[:, h % 2, :], tp[:, h % 4, 0:3 * P], ACT.Exp).then_inc(a_done, 1)
                if q + 1 < PAIRS:
                    ln_z(q + 1)
            turn(AH, G_Y2, range(4))
            hi(C_BR, [4])
            turn(AH, G_Y2, [4, 5])
            hi(C_BR, [5])
            turn(AH, G_Y2, [6, 7])
            hi(C_BR, range(6, 12))
            act.wait_ge(acc_free[0], A_BR[0])
            act.activation(PG[:, :, 7 * NT:8 * NT], PG[:, :, 7 * NT:8 * NT], ACT.Sigmoid).then_inc(last_gates, 1)
            with act.Fori(1, D // NT - 1) as i:
                hi(C_BR, range(4, 12), i, 8)
            hi(C_BR, range(28, 32))
            hi_and_turn(C_BR, 32, MH, G_M2, range(4))
            hi_and_turn(C_OUT2, 4, MH, G_M2, range(4, 8))
            hi(C_OUT2, range(8, 30))
            hi_and_turn(C_OUT2, 30, AH, G_F2, range(4), 4)
            hi(C_OUT2, range(34, 36))
            start(C_UP2, AH, G_F2, 4, slices_of(A_OUT2), N_F2)

            def up2(it, split):
                split(range(8, 12))
                act.wait_ge(inv_ready, N_F2 + 1)
                act.wait_ge(chunk_used, C_UP2 + 8 + 16 * it)
                for tb in range(TB):
                    s = act.activation(SG[:, tb, :], acc[:, 0, tb, :], ACT.Silu, scale=inv[:, N_F2, tb:tb + 1])
                s.then_inc(acc_free[0], 1)
                split(range(12, 20))
                split(range(20, 22))
                for b in range(2):
                    act.wait_ge(hb_turned, 2 * it + b + 1)
                    act.activation(BH[:, bass.ds(it * 4 + 2 * b, 2), :].rearrange("p a t -> p (a t)"), tp[:, b, :],
                                   ACT.Copy).then_inc(hb_hi, 1)
                split(range(22, 24))

            with act.Fori(0, FF // NT) as i:
                up2(i, lambda js: hi(C_UP2, js, i, 16))
            hi(C_DOWN2, range(8, 4 + FKT // 2))
            for n in range(1, D // NT):
                hi(C_DOWN2 + n * (FKT // 2), range(4, 8))
                squares(slices_of(A_DOWN2), N_END2, [n - 1])
                hi(C_DOWN2 + n * (FKT // 2), range(8, 4 + FKT // 2))
            squares(slices_of(A_DOWN2), N_END2, [D // NT - 1])
            sqrt_of(N_END2)
            act.wait_ge(inv_ready, N_END2 + 1)
            act.wait_ge(weighted, 3)
            for n in range(2):
                for tb in range(TB):
                    xs = X[:, tb, n * NT:(n + 1) * NT]
                    last = act.activation(xs, xs, ACT.Copy, scale=inv[:, N_END2, tb:tb + 1])
                last.then_inc(scaled_act, 1)

        @block.vector
        def _(dve):
            def lo(base, js, it=None, per=0):
                for j in js:
                    n = base + j
                    if n >= C_END:
                        continue
                    at = n if it is None else n + per * it
                    dve.wait_ge(hi_done, at + 1)
                    dve.tensor_tensor(WL[:, n % RING], WR[:, n % RING], WH[:, n % RING].bitcast(F32),
                                      ALU.subtract).then_inc(lo_done, 1)

            def turn(H, L, group, gs, w=None):
                for g in gs:
                    n = group + g
                    dve.wait_ge(turned_hi, n + 1)
                    if w is None:
                        last = dve.tensor_tensor(L[:, 2 * g:2 * g + 2, :].rearrange("p a t -> p (a t)"), tp[:, n % 4, :],
                                                 H[:, 2 * g:2 * g + 2, :].bitcast(F32).rearrange("p a t -> p (a t)"),
                                                 ALU.subtract)
                    else:
                        for k in range(2):
                            last = dve.scalar_tensor_tensor(
                                L[:, 2 * g + k, :], tp[:, n % 4, k * T:(k + 1) * T], nw[:, w, 2 * g + k:2 * g + k + 1],
                                H[:, 2 * g + k, :].bitcast(F32), ALU.mult, ALU.subtract)
                    last.then_inc(turned_lo, 1)

            def norm(n):
                dve.wait_ge(squared, 8 * (n + 1))
                dve.tensor_reduce(ssum[:], ss[:], AXX, ALU.add).then_inc(sums, 1)
                dve.wait_ge(sums, n + 1)
                dve.tensor_scalar(smean[:], ssum[:], 1.0 / D, EPS, ALU.mult, ALU.add).then_inc(mean, 1)
                dve.wait_ge(root, n + 1)
                dve.reciprocal(inv[:, n, :], sroot[:]).then_inc(inv_ready, 1)
                dve.wait_ge(inv_ready, n + 1)

            def scaled(dst, a, base, it, n):
                dve.wait_ge(chunk_used, base + 8 * (a + 1) + 16 * it)
                for tb in range(TB):
                    last = dve.tensor_scalar(dst(tb), acc[:, a, tb, :], inv[:, n, tb:tb + 1], None, ALU.mult)
                last.then_inc(acc_free[a], 1)

            def residual(n, a, end, it=0, per=0):
                dve.wait_ge(chunk_used, end + per * it)
                for tb in range(TB):
                    xs = X[:, tb, bass.ds(n * NT, NT)]
                    last = dve.tensor_tensor(xs, acc[:, a, tb, :], xs, ALU.add)
                last.then_inc(acc_free[a], 1)

            def lo_and_turn(base, j0, H, L, group, gs, w=None):
                for g in gs:
                    lo(base, [j0 + g - gs[0]])
                    turn(H, L, group, [g], w)

            def residuals(base, per, last, first=4):
                for n in range(D // NT):
                    if n < D // NT - 1:
                        lo(base + n * per, range(4 if n else first, 4 + per))
                    else:
                        last()
                    residual(n, n % 2, base + (n + 1) * per)

            dve.memset(nmax[:, 0, 0:1], 0.0).then_inc(acc_free[0], 1)
            dve.memset(WGH[:, KT * RANK:].bitcast(F32), 0.0)
            dve.memset(WGL[:, KT * RANK:].bitcast(F32), 0.0).then_inc(gate_pad, 1)
            dve.wait_ge(vec_turned, 1)
            dve.tensor_copy(vec[:, 0:6 * KT], acc_bank(3)[:, 0:6 * KT]).then_inc(vec_ready, 1)
            dve.wait_ge(vec_ready, 1)
            dve.tensor_tensor(nw[:, 3, :], nw[:, 3, :], nw[:, 5, :], ALU.mult).then_inc(vec_ready, 1)
            for n in range(4):
                turn(AH, AL, G_X1, [n], 0)
                lo(C_IN1, [n])
            lo_and_turn(C_IN1, 4, AH, AL, G_X1, range(4, 8), 0)
            norm(N_IN1)
            dve.wait_ge(gate_hi, 1)
            dve.tensor_tensor(WGL[:, 0:KT * RANK], WG[:].rearrange("p k n -> p (k n)"),
                              WGH[:, 0:KT * RANK].bitcast(F32), ALU.subtract).then_inc(gate_lo, 1)
            def in1_pair(i, first):
                lo(C_IN1, range(10 if first else 4, 12), i, 16)
                scaled(lambda tb: P1[:, tb, bass.ds(i * (2 * NT), NT)], 0, C_IN1, i, N_IN1)
                lo(C_IN1, range(12, 20), i, 16)
                scaled(lambda tb: P1[:, tb, bass.ds(i * (2 * NT) + NT, NT)], 1, C_IN1, i, N_IN1)

            lo(C_IN1, range(8, 10))
            dve.wait_ge(vec_turned, 2)
            dve.tensor_copy(vec[:, 6 * KT:], acc_bank(2)[:, 0:8 * FKT]).then_inc(acc_free[1], 1)
            in1_pair(0, True)
            with dve.Fori(1, 5) as i:
                in1_pair(i, False)

            def copy_pair(M, m, hp):
                if m % 2:
                    dve.wait_ge(qk_turned, m + 1)
                    dve.tensor_scalar(M[:, hp, 0, :], tp[:, m % 4, 0:T], HD ** -0.5, None, ALU.mult)
                    dve.tensor_copy(M[:, hp, 1, :], tp[:, m % 4, T:2 * T]).then_inc(qk_copied_v, 1)

            for q in range(PAIRS):
                lo(C_IN1, [84 + q])
                copy_pair(QK, q, q)
            scaled(lambda tb: P1[:, tb, 10 * NT:11 * NT], 0, C_IN1, 5, N_IN1)
            lo(C_IN1, [92])
            dve.wait_ge(gate_pe, 1)
            dve.tensor_copy(glT[:], tp[0:RANK, 0, 0:T]).then_inc(gate_v, 1)
            lo(C_IN1, range(93, 96))
            gv = [0]

            def step(ins):
                gv[0] += 1
                ins.then_inc(gla_v, 1)
                dve.wait_ge(gla_v, gv[0])

            dve.wait_ge(gla_in, 32)
            dve.wait_ge(gla_pe, 1)
            for tb in range(TB):
                step(dve.scalar_tensor_tensor(LG[:, tb, :], tp[:, 2 + tb, :], inv[:, N_IN1, tb:tb + 1], bgb[:],
                                              ALU.mult, ALU.add))
            step(dve.tensor_scalar(LM[:], LG[:], 0.0, None, ALU.min))
            step(dve.scalar_tensor_tensor(LG[:].rearrange("p a n -> p (a n)"), LM[:].rearrange("p a n -> p (a n)"), 2.0,
                                          LG[:].rearrange("p a n -> p (a n)"), ALU.mult, ALU.subtract))
            assert gv[0] == GV_NEG
            lo(C_IN1, range(96, 99))
            dve.wait_ge(gla_a, 2)
            step(dve.tensor_tensor(LM[:], LM[:], LG[:], ALU.subtract))

            def maxima(n, h, S, add_bias, R, M):
                dve.wait_ge(s_full, n + 1)
                if n >= 2:
                    dve.wait_ge(e_done, n - 1)
                add_bias(h, S[:, n % 2, :], tp[:, n % 2, :]).then_inc(s_read, 1)
                dve.wait_ge(s_read, n + 1)
                dve.tensor_reduce(R[:, h, 0:1], S[:, n % 2, 0:P], AXX, ALU.max)
                dve.tensor_reduce(R[:, h, 1:2], S[:, n % 2, P:3 * P], AXX, ALU.max).then_inc(s_max, 1)
                dve.wait_ge(s_max, n + 1)
                dve.tensor_scalar(M[:, h, :], R[:, h, :], -1.0, None, ALU.mult).then_inc(s_neg, 1)

            def band_bias(h, s, z):
                dve.tensor_tensor(s[:, 0:P], z[:, 0:P], BIAS[:, h, 2 * P - 1:P - 1:-1], ALU.add)
                return dve.tensor_tensor(s[:, P:3 * P], z[:, P:3 * P], BIAS[:, h, 3 * P - 1:P - 1:-1], ALU.add)

            def finish(R, C, dst, count):
                for qb in range(TB):
                    for g in range(2):
                        o = acc_bank(2 * qb + g).rearrange("p (h d) -> p h d", d=HD)
                        y = dst(qb, g).rearrange("p (h d) -> p h d", d=HD)
                        if C is None:
                            last = dve.tensor_copy(y, o)
                        else:
                            last = dve.tensor_tensor(y, o, wide(C[:, 8 * g:8 * g + 8, qb:qb + 1], [P, 8, HD]), ALU.mult)
                        last.then_inc(y_ready, 1)

            dve.wait_ge(bias_masked, 1)
            maxima(0, 0, SB, band_bias, rmax, nmax)
            scaled(lambda tb: P1[:, tb, 11 * NT:12 * NT], 1, C_IN1, 5, N_IN1)
            step(dve.tensor_scalar(LA[:], LM[:], 1.0 / TAU, None, ALU.mult))
            assert gv[0] == GV_LA
            for h in range(1, HEADS):
                maxima(h, h, SB, band_bias, rmax, nmax)
                if h == 1:
                    lo(C_IN1, [99])
            dve.wait_ge(e_done, HEADS)
            dve.reciprocal(rrec[:], rsum[:]).then_inc(rec_done, 1)
            dve.wait_ge(rec_done, 1)
            dve.wait_ge(pv_done, HEADS)
            finish(rsum, rrec, lambda qb, g: P1[:, qb, QA1 + g * NT:QA1 + (g + 1) * NT], 0)

            dve.wait_ge(gla_a, 3)
            step(dve.tensor_tensor(KE[:], KE[:], P1[:, :, KG1:KG1 + GLA_KW], ALU.mult))
            assert gv[0] == GV_KE
            dve.wait_ge(gla_pe, 2)
            dve.wait_ge(gla_a, 4)
            for h in range(GLA_HEADS):
                step(dve.scalar_tensor_tensor(QD[:, h, :], tp[:, h, 0:T], GLA_DK ** -0.5, EB[:, h, :], ALU.mult, ALU.mult))
                step(dve.tensor_tensor(KI[:, h, :], tp[:, h, T:2 * T], EN[:, h, :], ALU.mult))
            assert gv[0] == GV_QK
            for c in range(3):
                dve.wait_ge(gla_pe, 5 + c)
                for h in range(GLA_HEADS):
                    upd = acc_bank(2 * (c % 2) + h // 2)[:, (h % 2) * GLA_DV:(h % 2 + 1) * GLA_DV]
                    if c == 0:
                        step(dve.tensor_copy(ST[:, 0, h, :], upd))
                    else:
                        step(dve.scalar_tensor_tensor(ST[:, c, h, :], ST[:, c - 1, h, :],
                                                      EB[:, h, (c + 1) * LOOK - 1:(c + 1) * LOOK], upd,
                                                      ALU.mult, ALU.add))
                if c == 0:
                    assert gv[0] == GV_ST1
            assert gv[0] == GV_ST2
            dve.wait_ge(gnw_in, 16)
            dve.wait_ge(gla_a, GA_SILU)
            for tb in range(TB):
                step(dve.tensor_tensor(SR[:, tb, :].rearrange("p (h d) -> p h d", d=GLA_DV),
                                       SR[:, tb, :].rearrange("p (h d) -> p h d", d=GLA_DV),
                                       wide(gnw[:, None, :], [P, GLA_HEADS, GLA_DV]), ALU.mult))
            turn(ZH, ZL, G_Y1, range(4))
            dve.wait_ge(gla_a, 14)
            step(dve.tensor_scalar(osm[:], osq[:], 1.0 / GLA_DV, EPS, ALU.mult, ALU.add))
            assert gv[0] == GV_OSM
            dve.wait_ge(gla_a, 15)
            step(dve.reciprocal(oiv[:], osr[:]))
            for tb in range(TB):
                for h in range(GLA_HEADS):
                    cols = slice(h * GLA_DV, (h + 1) * GLA_DV)
                    step(dve.scalar_tensor_tensor(P1[:, tb, RG1 + h * GLA_DV:RG1 + (h + 1) * GLA_DV],
                                                  acc_bank(2 * tb + h // 2)[:, (h % 2) * GLA_DV:(h % 2 + 1) * GLA_DV],
                                                  oiv[:, tb, h:h + 1], SR[:, tb, cols], ALU.mult, ALU.mult))
            assert gv[0] == GV_END
            lo_and_turn(C_OUT1, 4, ZH, ZL, G_Y1, range(4, 8))
            def last_lo(base, group, w):
                def go():
                    lo(base, range(28, 30))
                    lo_and_turn(base, 30, AH, AL, group, range(4), w)
                    lo(base, range(34, 36))
                return go

            residuals(C_OUT1, 8, last_lo(C_OUT1, G_F1, 1), first=8)
            lo_and_turn(C_UP1, 4, AH, AL, G_F1, range(4, 8), 1)
            norm(N_F1)

            def taps(a, b, it):
                dve.wait_ge(c_init, 4 * it + 2 * a + b + 1)
                for tap, back in ((1, 1), (0, 2)):
                    if back == 2:
                        dve.wait_ge(tap1, 4 * it + 2 * a + b + 1)
                    for k in range(2):
                        fb = 2 * b + k
                        f = it * 4 + (a * FKT + fb)
                        last = dve.scalar_tensor_tensor(CV[:, a, fb, back:T], tp[:, 2 * a + b, k * T:(k + 1) * T - back],
                                                        cw[:, tap, bass.ds(f, 1)], CV[:, a, fb, back:T],
                                                        ALU.mult, ALU.add)
                    last.then_inc(tap1 if back == 1 else conv_done, 1)

            def up1(it, split):
                split(range(8, 14))
                taps(0, 0, it)
                split(range(14, 15))
                taps(0, 1, it)
                split(range(15, 20))
                split(range(20, 22))
                taps(1, 0, it)
                split(range(22, 23))
                taps(1, 1, it)
                split(range(23, 24))
                dve.wait_ge(gelu_done, it + 1)
                dve.wait_ge(conv_done, 4 * it + 4)
                dve.tensor_tensor(CV[:, 0], CV[:, 0], CV[:, 1], ALU.mult).then_inc(h_ready, 1)
                dve.wait_ge(h_hi, it + 1)
                dve.tensor_tensor(BL[:, bass.ds(it * 4, 4), :], CV[:, 0], BH[:, bass.ds(it * 4, 4), :].bitcast(F32),
                                  ALU.subtract).then_inc(h_lo, 1)

            with dve.Fori(0, FF // NT) as i:
                up1(i, lambda js: lo(C_UP1, js, i, 16))
            def last_down():
                lo(C_DOWN1, range(70, 81))
                turn(PTH, PTL, G_P, [0])
                lo(C_DOWN1, [81])
                lo_and_turn(C_DOWN1, 82, AH, AL, G_PLE, range(4), 2)
                lo(C_DOWN1, range(86, 92))

            residuals(C_DOWN1, FKT // 2, last_down, first=8)
            for n in range(D // NT):
                dve.wait_ge(chunk_used, C_PROJ + n + 1)
                for tb in range(TB):
                    last = dve.tensor_copy(PP[:, tb, n * NT:(n + 1) * NT], acc[:, n % 2, tb, :])
                last.then_inc(acc_free[n % 2], 1)
                lo(C_PROJ, [4 + n])
            lo_and_turn(C_PLE, 4, AH, AL, G_PLE, range(4, 8), 2)
            norm(N_PLE)

            def gated(n):
                dve.wait_ge(acc_free[n % 2], A_PLE + n // 2 + 1)
                cols = slice(n * NT, (n + 1) * NT)
                dve.tensor_tensor(GT[:], GT[:], PP[:, :, cols], ALU.mult).then_inc(g_mul, 1)
                dve.wait_ge(g_mul, n + 1)
                dve.tensor_tensor(X[:, :, cols], X[:, :, cols], GT[:], ALU.add).then_inc(x_scaled, 1)

            for n in range(D // NT - 1):
                lo(C_PLE + 8 * n, range(8 if n == 0 else 4, 12))
                gated(n)
            lo(C_PLE, range(28, 31))
            lo_and_turn(C_PLE, 31, XH, XL, G_X2, range(4), 3)
            gated(D // NT - 1)
            lo(C_PLE, [35])
            lo_and_turn(C_IN2, 4, XH, XL, G_X2, range(4, 8), 3)
            lo(C_IN2, [8])
            norm(N_END1)
            dve.wait_ge(fw_in, 16)
            for n in range(D // NT):
                lo(C_IN2, [9 + n])
                cols = slice(n * NT, (n + 1) * NT)
                for tb in range(TB):
                    last = dve.scalar_tensor_tensor(X[:, tb, cols], X[:, tb, cols], inv[:, N_END1, tb:tb + 1],
                                                    fw[:, cols], ALU.mult, ALU.mult)
                last.then_inc(x_scaled, 1)
            lo(C_IN2, [13])
            norm(N_IN2)
            dve.tensor_tensor(inv[:, N_IN2, :], inv[:, N_IN2, :], inv[:, N_END1, :], ALU.mult).then_inc(inv_both, 1)
            dve.wait_ge(inv_both, 1)
            def to_pq(n):
                return lambda tb: PQ[:, tb, bass.ds(n * NT, NT)]

            def in2_pair(i, first):
                if not first:
                    lo(C_IN2, range(4, 12), i, 16)
                scaled(to_pq(2 * i), 0, C_IN2, i, N_IN2)
                lo(C_IN2, range(14 if first else 12, 20), i, 16)
                scaled(to_pq(2 * i + 1), 1, C_IN2, i, N_IN2)

            in2_pair(0, True)
            with dve.Fori(1, 4) as i:
                in2_pair(i, False)
            lo(C_IN2 + 64, range(4, 12))
            scaled(to_pq(8), 0, C_IN2, 4, N_IN2)
            with dve.Fori(0, 3) as i:
                lo(C_IN2 + 64, range(12, 28), i, 16)
            for q in range(PAIRS):
                lo(C_IN2, [124 + q])
                copy_pair(QKB, PAIRS + q, q)
            for q in range(PAIRS - 1):
                lo(C_IN2, [132 + q])
                m = 2 * PAIRS + q
                if q in (1, 3):
                    dve.wait_ge(qk_turned, m + 1)
                    dve.tensor_scalar(QT2[:, 2 * q:2 * q + 2, :].rearrange("p a t -> p (a t)"), tp[:, m % 4, :],
                                      HD ** -0.5, None, ALU.mult).then_inc(qk_copied_v, 1)
                elif q == 5:
                    dve.wait_ge(qk_turned, m + 1)
                    dve.tensor_copy(KT2[:, 2:4, :].rearrange("p a t -> p (a t)"),
                                    tp[:, m % 4, :]).then_inc(qk_copied_v, 1)

            def window_bias(h, s, z):
                slope = -(2.0 ** (-8.0 * (h + 1) / HEADS))
                dve.scalar_tensor_tensor(s[:, 0:P], dist[:, P:2 * P], slope, z[:, 0:P], ALU.mult, ALU.add)
                return dve.scalar_tensor_tensor(s[:, P:3 * P], dist[:], slope, z[:, P:3 * P], ALU.mult, ALU.add)

            dve.wait_ge(sk_in, 16)
            dve.wait_ge(kd_done, 3)
            for h in range(HEADS):
                if h == 1:
                    scaled(lambda tb: PG[:, tb, 7 * NT:8 * NT], 0, C_IN2, 8, N_IN2)
                if h == 2:
                    lo(C_IN2, [139])
                n = HEADS + h
                dve.wait_ge(s_full, n + 1)
                dve.wait_ge(e_done, n - 1)
                window_bias(h, SB2[:, n % 2, :], tp[:, n % 2, :]).then_inc(s_read, 1)
                dve.wait_ge(s_read, n + 1)
                dve.tensor_reduce(rmax2[:, h, 0:1], SB2[:, n % 2, 0:P], AXX, ALU.max)
                dve.tensor_reduce(rmax2[:, h, 1:2], SB2[:, n % 2, P:3 * P], AXX, ALU.max).then_inc(s_max, 1)
                dve.wait_ge(s_max, n + 1)
                dve.tensor_scalar(nmax2[:, h, :], rmax2[:, h, :], sk[:, h:h + 1], -1.0, ALU.max,
                                  ALU.mult).then_inc(s_neg, 1)
            def softplus_argument(q):
                for h in (2 * q, 2 * q + 1):
                    i = h % 4
                    z = tp[:, i, 0:3 * P]
                    dve.wait_ge(z_full, h + 1)
                    dve.tensor_scalar(SM[:, i, :], z, 0.0, None, ALU.max).then_inc(m_done, 1)
                    dve.wait_ge(m_done, h + 1)
                    dve.scalar_tensor_tensor(SE[:, i, :], SM[:, i, :], -2.0, z, ALU.mult, ALU.add).then_inc(z_read, 1)

            dve.wait_ge(s_neg, 2 * HEADS)
            dve.wait_ge(e_done, 2 * HEADS)
            dve.tensor_tensor(sk2[:], nmax2[:], wide(sk[:, :, None], [P, HEADS, 2]), ALU.add).then_inc(sink_v, 1)
            dve.wait_ge(sink_a, 1)
            dve.tensor_tensor(rsum2[:], rsum2[:], sk2[:], ALU.add).then_inc(sink_v, 1)
            dve.wait_ge(sink_v, 2)
            dve.reciprocal(rrec2[:], rsum2[:]).then_inc(rec_done, 1)
            dve.wait_ge(rec_done, 2)
            dve.wait_ge(pv_done, 2 * HEADS)
            softplus_argument(0)
            finish(rsum2, rrec2, lambda qb, g: PQ[:, qb, QA2 + g * NT:QA2 + (g + 1) * NT], 4)
            softplus_argument(1)
            for q in range(PAIRS):
                for h in (2 * q, 2 * q + 1):
                    dve.wait_ge(ln_done, h + 1)
                    dve.tensor_tensor(SE[:, h % 4, :], SE[:, h % 4, :], SM[:, h % 4, :], ALU.add).then_inc(sp_done, 1)
                if q + 2 < PAIRS:
                    softplus_argument(q + 2)
            dve.wait_ge(stick_pv, HEADS)
            finish(None, None, lambda qb, g: PQ[:, qb, QB2 + g * NT:QB2 + (g + 1) * NT], 8)
            turn(AH, AL, G_Y2, range(4))
            lo(C_BR, [4])
            turn(AH, AL, G_Y2, [4, 5])
            lo(C_BR, [5])
            turn(AH, AL, G_Y2, [6, 7])
            lo(C_BR, range(6, 8))
            dve.wait_ge(acc_free[0], A_BR[0])
            dve.wait_ge(acc_free[1], A_BR[1])

            def merge(n, second):
                ga, gb = PG[:, :, bass.ds(n * NT, NT)], PG[:, :, bass.ds(n * NT + D, NT)]
                dve.wait_ge(chunk_used, 8 * n + (C_BR + 4))
                dve.tensor_tensor(ga, acc[:, 0], ga, ALU.mult).then_inc(acc_free[0], 1)
                second()
                dve.wait_ge(chunk_used, 8 * n + (C_BR + 8))
                dve.tensor_tensor(gb, acc[:, 1], gb, ALU.mult).then_inc(acc_free[1], 1)
                dve.wait_ge(acc_free[0], n + (A_BR[0] + 1))
                dve.wait_ge(acc_free[1], n + (A_BR[1] + 1))
                dve.tensor_tensor(ga, ga, gb, ALU.add).then_inc(m_ready, 1)

            merge(0, lambda: lo(C_BR, range(8, 12)))
            with dve.Fori(1, D // NT - 1) as i:
                lo(C_BR, range(4, 8), i, 8)
                merge(i, lambda: lo(C_BR, range(8, 12), i, 8))
            lo(C_BR, range(28, 32))
            dve.wait_ge(last_gates, 1)
            merge(D // NT - 1, lambda: lo_and_turn(C_BR, 32, MH, ML, G_M2, range(4)))
            lo_and_turn(C_OUT2, 4, MH, ML, G_M2, range(4, 8))
            residuals(C_OUT2, 8, last_lo(C_OUT2, G_F2, 4), first=8)
            lo_and_turn(C_UP2, 4, AH, AL, G_F2, range(4, 8), 4)
            norm(N_F2)

            def up2(it, split):
                split(range(8, 20))
                dve.wait_ge(chunk_used, C_UP2 + 16 + 16 * it)
                dve.wait_ge(acc_free[0], A_UP2[0] + it + 1)
                for tb in range(TB):
                    s = dve.scalar_tensor_tensor(HB[:, tb, :], acc[:, 1, tb, :], inv[:, N_F2, tb:tb + 1], SG[:, tb, :],
                                                 ALU.mult, ALU.mult)
                s.then_inc(acc_free[1], 1)
                split(range(20, 22))
                for b in range(2):
                    dve.wait_ge(hb_hi, 2 * it + b + 1)
                    cols = bass.ds(it * 4 + 2 * b, 2)
                    dve.tensor_tensor(BL[:, cols, :].rearrange("p a t -> p (a t)"), tp[:, b, :],
                                      BH[:, cols, :].bitcast(F32).rearrange("p a t -> p (a t)"),
                                      ALU.subtract).then_inc(hb_lo, 1)
                split(range(22, 24))

            with dve.Fori(0, FF // NT) as i:
                up2(i, lambda js: lo(C_UP2, js, i, 16))
            for n in range(D // NT):
                if n == 0:
                    lo(C_DOWN2, range(8, 4 + FKT // 2))
                else:
                    lo(C_DOWN2 + n * (FKT // 2), range(4, 12))
                    if n == 1:
                        dve.wait_ge(fg_in, 16)
                    dve.wait_ge(squared, 8 * N_END2 + 2 * n)
                    xs = X[:, :, (n - 1) * NT:n * NT]
                    dve.tensor_tensor(xs, xs, wide(fw2[:, None, (n - 1) * NT:n * NT], [P, TB, NT]),
                                      ALU.mult).then_inc(weighted, 1)
                    lo(C_DOWN2 + n * (FKT // 2), range(12, 4 + FKT // 2))
                residual(n, n % 2, C_DOWN2 + (n + 1) * (FKT // 2))
            norm(N_END2)
            for tb in range(TB):
                xs = X[:, tb, 3 * NT:]
                last = dve.scalar_tensor_tensor(xs, xs, inv[:, N_END2, tb:tb + 1], fw2[:, 3 * NT:], ALU.mult, ALU.mult)
            last.then_inc(scaled_dve, 1)
            for tb in range(TB):
                xs = X[:, tb, 2 * NT:3 * NT]
                last = dve.tensor_scalar(xs, xs, inv[:, N_END2, tb:tb + 1], None, ALU.mult)
            last.then_inc(scaled_dve, 1)


_NAMES = ['x', 'p', 'norm_mix_w', 'w_in', 'att_rel_bias', 'w_gla_gate_up', 'b_gla_gate', 'gla_norm_w', 'w_out',
          'norm_ffn_w', 'w_ffn_up', 'w_ffn_conv', 'b_ffn_conv', 'w_ffn_down', 'norm_ple_w', 'w_ple_gate',
          'w_ple_proj', 'final_norm_w', 'norm_mix_g_2', 'w_in_2', 'sink_logits_2', 'w_branch_a_2', 'w_branch_b_2',
          'w_out_2', 'norm_ffn_g_2', 'w_ffn_in_2', 'w_ffn_down_2', 'norm_final_g_2']


def kernel(**inputs):
    import numpy as _np
    import concourse.bacc as _bacc
    from concourse import mybir as _mybir
    from concourse.bass_utils import run_bass_kernel_spmd as _run

    nc = _bacc.Bacc("TRN2", target_bir_lowering=False, num_devices=1)
    arrays, args = {}, []
    for name in _NAMES:
        a = _np.ascontiguousarray(inputs[name])
        while a.ndim > 1 and a.shape[0] == 1:
            a = a[0]
        arrays[f"in_{name}_dram"] = a
        args.append(nc.dram_tensor(f"in_{name}_dram", a.shape, _mybir.dt.from_np(a.dtype), kind="ExternalInput").ap())
    args.append(nc.dram_tensor("out_0_dram", (T, D), F32, kind="ExternalOutput").ap())
    two_blocks_kernel(nc, *args)
    r = _run(nc, [arrays], core_ids=[0])
    return r.results[0]["out_0_dram"].reshape(1, T, D)
```
